# Optimizing a Trainium2 kernel written in Bass

```python
import math
import jax, jax.numpy as jnp
from jax import lax
import numpy as np

D_MODEL = 1024
BATCH = 1
SEQ = 2048
DEPTH = 1

PLE_DIM = 256
HEAD_DIM = 64
ATTN_HEADS = 8
KV_HEADS = 2
ATTN_WIDTH = ATTN_HEADS * HEAD_DIM
IDX_HEADS = 4
IDX_DIM = 64
TOPK_MAX = 256
Q_BLOCK = 128
POOL_WINDOWS = (2, 4, 8, 16)
POOL_GROUPS = len(POOL_WINDOWS)
POOL_WIDTH = D_MODEL - ATTN_WIDTH
POOL_GROUP_DIM = POOL_WIDTH // POOL_GROUPS
MIX_WIDTH = ATTN_WIDTH + POOL_WIDTH
D_FF = 4 * D_MODEL
ROPE_THETA = 500000.0
ROT_DIM = HEAD_DIM // 4
EPS = 1e-6
ATTN_SCALE = HEAD_DIM ** -0.5
IDX_SCALE = IDX_DIM ** -0.5
IN_WIDTHS = (ATTN_HEADS * HEAD_DIM,
             KV_HEADS * HEAD_DIM,
             KV_HEADS * HEAD_DIM,
             IDX_HEADS * IDX_DIM,
             IDX_DIM,
             IDX_HEADS,
             POOL_WIDTH)
IN_WIDTH = sum(IN_WIDTHS)
IN_SPLITS = tuple(int(v) for v in np.cumsum(IN_WIDTHS)[:-1])

kernel_name = "hybrid_dsa_pool_parallel_block"

def rmsnorm(x, g):
    xf = x.astype(jnp.float32)
    y = xf * lax.rsqrt(jnp.mean(xf * xf, axis=-1, keepdims=True) + EPS)
    return (y * g.astype(jnp.float32)).astype(x.dtype)

def rope_tables(positions):
    inv_freq = ROPE_THETA ** (-jnp.arange(0, ROT_DIM, 2, dtype=jnp.float32) / ROT_DIM)
    ang = positions.astype(jnp.float32)[..., None] * inv_freq
    return jnp.cos(ang)[:, :, None, :], jnp.sin(ang)[:, :, None, :]

def rope_partial(x, cos, sin):
    half = ROT_DIM // 2
    x1, x2, rest = x[..., :half], x[..., half:ROT_DIM], x[..., ROT_DIM:]
    c, s = cos.astype(x.dtype), sin.astype(x.dtype)
    return jnp.concatenate([x1 * c - x2 * s, x2 * c + x1 * s, rest], axis=-1)

def dsa_attention(q, k, v, q_idx, k_idx, w_idx):
    B, S, H, Dh = q.shape
    G = k.shape[2]
    R = H // G
    n_keep = min(TOPK_MAX, S // 4)
    nb = S // Q_BLOCK
    key_pos = jnp.arange(S)
    q_pos = key_pos.reshape(nb, Q_BLOCK)
    gather = jax.vmap(lambda table, idx: table[idx])

    def to_blocks(a):
        return a.reshape((B, nb, Q_BLOCK) + a.shape[2:]).swapaxes(0, 1)

    def block(args):
        qb, qib, wb, tq = args
        logits = jnp.einsum('bqhd,bsd->bqhs', qib, k_idx).astype(jnp.float32) * IDX_SCALE
        score = jnp.einsum('bqh,bqhs->bqs', wb.astype(jnp.float32), jax.nn.relu(logits))
        causal = key_pos[None, :] <= tq[:, None]
        score = jnp.where(causal[None], score, -jnp.inf)
        _, sel = lax.top_k(score, n_keep)
        valid = sel <= tq[None, :, None]
        kg = gather(k, sel)
        vg = gather(v, sel)
        qg = qb.reshape(B, Q_BLOCK, G, R, Dh)
        s = jnp.einsum('bqgrd,bqkgd->bqgrk', qg, kg).astype(jnp.float32) * ATTN_SCALE
        s = jnp.where(valid[:, :, None, None, :], s, -jnp.inf)
        pr = jax.nn.softmax(s, axis=-1).astype(vg.dtype)
        o = jnp.einsum('bqgrk,bqkgd->bqgrd', pr, vg)
        return o.reshape(B, Q_BLOCK, H * Dh)

    out = lax.map(block, (to_blocks(q), to_blocks(q_idx), to_blocks(w_idx), q_pos))
    return out.swapaxes(0, 1).reshape(B, S, H * Dh)

def pool_mixer(u, w_grp, scale):
    B, S, C = u.shape
    ug = u.reshape(B, S, POOL_GROUPS, POOL_GROUP_DIM)
    csum = jnp.cumsum(ug.astype(jnp.float32), axis=1)
    t = jnp.arange(S)
    means = []
    for g, w in enumerate(POOL_WINDOWS):
        cg = csum[:, :, g]
        lag = jnp.pad(cg, ((0, 0), (w, 0), (0, 0)))[:, :S]
        cnt = jnp.minimum(t + 1, w).astype(jnp.float32)[None, :, None]
        means.append((cg - lag) / cnt)
    mean = jnp.stack(means, axis=2)
    r = (mean - ug.astype(jnp.float32)).astype(u.dtype)
    y = jnp.einsum('bsgc,gcd->bsgd', r, w_grp)
    return y.reshape(B, S, C) * scale

def setup_inputs(seed: int = 0) -> dict:
    key = jax.random.key(seed)
    ks = jax.random.split(key, 20)
    f32 = jnp.float32

    def nrm(k, shape, fan_in):
        return jax.random.normal(k, shape, f32) * (fan_in ** -0.5)

    def gain(k, n):
        return 1.0 + 0.05 * jax.random.normal(k, (DEPTH, n), f32)

    x = jax.random.normal(ks[0], (BATCH, SEQ, D_MODEL), f32)
    p = jax.random.normal(ks[1], (DEPTH, BATCH, SEQ, PLE_DIM), f32)
    offset = jax.random.randint(ks[2], (BATCH, 1), 0, 4096, dtype=jnp.int32)
    positions = (offset + jnp.arange(SEQ, dtype=jnp.int32)[None, :]).astype(jnp.int32)
    return {
        "x": x,
        "p": p,
        "positions": positions,
        "g_mix_pre": gain(ks[3], D_MODEL),
        "w_in": nrm(ks[4], (DEPTH, D_MODEL, IN_WIDTH), D_MODEL),
        "w_pool": nrm(ks[5], (DEPTH, POOL_GROUPS, POOL_GROUP_DIM, POOL_GROUP_DIM), POOL_GROUP_DIM),
        "pool_scale": 1.0 + 0.1 * jax.random.normal(ks[6], (DEPTH, POOL_WIDTH), f32),
        "w_o": nrm(ks[7], (DEPTH, MIX_WIDTH, D_MODEL), MIX_WIDTH),
        "g_mix_post": gain(ks[8], D_MODEL),
        "g_mlp_pre": gain(ks[9], D_MODEL),
        "w_up": nrm(ks[10], (DEPTH, D_MODEL, D_FF), D_MODEL),
        "w_down": nrm(ks[11], (DEPTH, D_FF, D_MODEL), D_FF),
        "g_mlp_post": gain(ks[12], D_MODEL),
        "w_ple_gate": nrm(ks[13], (DEPTH, D_MODEL, D_MODEL), D_MODEL),
        "w_ple_proj": nrm(ks[14], (DEPTH, PLE_DIM, D_MODEL), PLE_DIM),
        "g_ple_post": gain(ks[15], D_MODEL),
    }

def reference(x, p, positions, g_mix_pre, w_in, w_pool, pool_scale, w_o, g_mix_post,
              g_mlp_pre, w_up, w_down, g_mlp_post, w_ple_gate, w_ple_proj, g_ple_post):
    B, S, _ = x.shape
    cos, sin = rope_tables(positions)
    h = x
    for i in range(DEPTH):
        hn = rmsnorm(h, g_mix_pre[i])
        z = hn @ w_in[i]
        zq, zk, zv, zqi, zki, zw, zp = jnp.split(z, IN_SPLITS, axis=-1)
        q = rope_partial(zq.reshape(B, S, ATTN_HEADS, HEAD_DIM), cos, sin)
        k = rope_partial(zk.reshape(B, S, KV_HEADS, HEAD_DIM), cos, sin)
        v = zv.reshape(B, S, KV_HEADS, HEAD_DIM)
        qi = rope_partial(zqi.reshape(B, S, IDX_HEADS, IDX_DIM), cos, sin)
        ki = rope_partial(zki.reshape(B, S, 1, IDX_DIM), cos, sin)[:, :, 0]
        wi = zw * (IDX_HEADS ** -0.5)
        attn_out = dsa_attention(q, k, v, qi, ki, wi)
        pool_out = pool_mixer(zp, w_pool[i], pool_scale[i])
        mix = jnp.concatenate([attn_out, pool_out], axis=-1) @ w_o[i]
        h = h + rmsnorm(mix, g_mix_post[i])
        hn = rmsnorm(h, g_mlp_pre[i])
        m = jnp.square(jax.nn.relu(hn @ w_up[i])) @ w_down[i]
        h = h + rmsnorm(m, g_mlp_post[i])
        gate = jax.nn.sigmoid(h @ w_ple_gate[i])
        e = p[i] @ w_ple_proj[i]
        h = h + rmsnorm(gate * e, g_ple_post[i])
    return h


_drawn_inputs = setup_inputs


def setup_inputs(seed=0):
    import zlib

    import numpy as np

    out = dict(_drawn_inputs(seed))
    spreads = {}
    factors = {}
    for name, (base, spread) in spreads.items():
        noise = np.random.default_rng([zlib.crc32(name.encode()), seed]).standard_normal(out[name].shape)
        drawn = base * np.exp(spread * noise) if base else spread * noise
        out[name] = __import__('jax').numpy.asarray(drawn.astype(out[name].dtype))
    for name, factor in factors.items():
        out[name] = (out[name] * factor).astype(out[name].dtype)
    return out
```

```python
from contextlib import ExitStack

import numpy as np

import concourse.bass as bass
from concourse import mybir

P = 128
F32 = mybir.dt.float32
I32 = mybir.dt.int32
ALU = mybir.AluOpType
ACT = mybir.ActivationFunctionType
AX_X = mybir.AxisListType.X

HEAD = 64
Q_HEADS = 8
KV_HEADS = 2
IDX_HEADS = 4
KEEP = 256
WINDOWS = (2, 4, 8, 16)
HALO = 16
ROT_HALF = 8
THETA = 500000.0
EPS = 1e-6
MASKED = -1.0e30
TAKEN = -3.0e38
ROUND = 12582912.0
TWO_PI = (6.28125, 1.9340515136718750e-3, 2 * np.pi - 6.28125 - 1.9340515136718750e-3)
PI_SAFE = 3.1415925

GROUPS = [(0, 2, 256)] + [(t, 2, 128 * (t + 2)) for t in range(2, 16, 2)]


def blocks_of(keys):
    return [(o, min(512, keys - o)) for o in range(0, keys, 512)]


class Count:

    def __init__(self, per_group):
        self.per = per_group
        self.before = [sum(per_group[g] * GROUPS[g][1] for g in range(n)) for n in range(len(GROUPS))]

    def at(self, g, t, k):
        return self.before[g] + t * self.per[g] + k

    def ring(self, g, t, k, depth):
        return self.at(g, t, max(k + 1 - depth, 0))


def hybrid_block(nc, x, p, positions, g_mix_pre, w_in, w_pool, pool_scale, w_o, g_mix_post,
                 g_mlp_pre, w_up, w_down, g_mlp_post, w_ple_gate, w_ple_proj, g_ple_post, out):
    S, D = x.shape[1], x.shape[2]
    T = S // P
    K = D // P
    W_IN = w_in.shape[2]
    FF = w_up.shape[2]
    PLE = p.shape[3]
    KP = PLE // P
    G = len(WINDOWS)
    Z_A, Z_B = 512, 1024
    Z_POOL = W_IN - G * P
    Z_C = Z_POOL - Z_B
    CH = 512
    CT = CH // P
    NCH = S // CH
    FT = FF // P
    assert (S, D, T, K, FT) == (2048, 1024, 16, 8, 32) and Z_C == HEAD + IDX_HEADS

    h2_dram = nc.dram_tensor("h2_scratch", [S, D], F32, kind="Internal").ap()
    hnT_dram = nc.dram_tensor("hnT_scratch", [P, K, S], F32, kind="Internal").ap()

    with ExitStack() as ctx:
        def alloc(stack):
            return lambda name, shape, dt=F32: stack.enter_context(nc.sbuf_tensor(name, shape, dt))

        def sem(name):
            return ctx.enter_context(nc.semaphore(name))

        bank = ctx.enter_context(nc.psum_tensor("bank", [P, 8, 512], F32))
        sb = alloc(ctx)
        ident = sb("ident", [P, P])
        minus_half = sb("minus_half", [P, 1])
        g_mlp_col = sb("g_mlp_col", [P, K])

        attn_stack = ExitStack()
        sbB0 = alloc(attn_stack)
        kq = sbB0("kq", [P, 4, S])
        qT = sbB0("qT", [P, 4, S])
        values = sbB0("values", [P, T, P])
        poolT = sbB0("poolT", [P, G, S])
        w_idx = sbB0("w_idx", [P, T, IDX_HEADS])
        causal = sbB0("causal", [P, 384])

        proj_stack = ExitStack()
        sbA = alloc(proj_stack)
        w_in_sb = sbA("w_in_sb", [P, K, W_IN])
        w_pool_sb = sbA("w_pool_sb", [P, G, P])
        g_pre_col = sbA("g_pre_col", [P, K])
        pool_scale_col = sbA("pool_scale_col", [P, G])
        x_in = sbA("x_in", [P, 2, D])
        xn = sbA("xn", [P, D])
        hnT = sbA("hnT", [P, K, P])
        zs = sbA("zs", [P, 2, 16, HEAD])
        zp = sbA("zp", [P, G, HALO + P])
        sum_a = sbA("sum_a", [P, G, HALO + P])
        sum_b = sbA("sum_b", [P, G, HALO + P])
        edge = sbA("edge", [P, G, HALO])
        r_pool = sbA("r_pool", [P, G, P])
        rot = sbA("rot", [P, 4, 15, ROT_HALF])
        pos_i = sbA("pos_i", [P, T], I32)
        pos_f = sbA("pos_f", [P, T])
        freq = sbA("freq", [P, ROT_HALF])
        angle = sbA("angle", [P, T, ROT_HALF])
        turns = sbA("turns", [P, 2, T, ROT_HALF])
        trig = sbA("trig", [P, 2, T, ROT_HALF])
        ss = sbA("ss", [P, 2])
        ms = sbA("ms", [P, 2])
        rstd = sbA("rstd", [P, 2])
        proj_stack.close()

        tile_stack = ExitStack()
        sbB = alloc(tile_stack)
        wo_sb = sbB("wo_sb", [P, K, D])
        score = sbB("score", [P, S])
        work = sbB("work", [P, S])
        probs = sbB("probs", [P, 2, S])
        relu = sbB("relu", [P, 2, 512])
        probsT = sbB("probsT", [P, 2, 512])
        qT_t = sbB("qT_t", [P, 4, P])
        qiT_t = sbB("qiT_t", [P, 2, P])
        mixT_t = sbB("mixT_t", [P, K, P])
        o_sb = sbB("o_sb", [P, Q_HEADS, HEAD])
        x_t = sbB("x_t", [P, D])
        h2_t = sbB("h2_t", [P, D])
        hn2_t = sbB("hn2_t", [P, D])
        hn2T_t = sbB("hn2T_t", [P, K, P])
        g_post_row = sbB("g_post_row", [P, D])
        top8 = sbB("top8", [P, 8])
        block_max = sbB("block_max", [P, 2, 4])
        neg_max = sbB("neg_max", [P, Q_HEADS])
        denom = sbB("denom", [P, Q_HEADS])
        inv_denom = sbB("inv_denom", [P, Q_HEADS])
        ssB = sbB("ssB", [P, 4])
        msB = sbB("msB", [P, 2])
        rstdB = sbB("rstdB", [P, 2])
        tile_stack.close()
        attn_stack.close()

        mlp_stack = ExitStack()
        sbC = alloc(mlp_stack)
        ring = sbC("ring", [P, 4, 2048])
        hidden = sbC("hidden", [P, FT, CH])
        hn2T = sbC("hn2T", [P, K, CH])
        h2 = sbC("h2", [P, CT, D])
        w_gate_sb = sbC("w_gate_sb", [P, K, D])
        w_ple_sb = sbC("w_ple_sb", [P, KP, D])
        g_mlp_row = sbC("g_mlp_row", [P, D])
        g_ple_row = sbC("g_ple_row", [P, D])
        p_in = sbC("p_in", [P, CT, PLE])
        pT = sbC("pT", [P, KP, CH])
        m_t = sbC("m_t", [P, D])
        h3T = sbC("h3T", [P, K, P])
        sig = sbC("sig", [P, D])
        out_t = sbC("out_t", [P, D])
        junk = sbC("junk", [P, D])
        ssC = sbC("ssC", [P, 4])
        msC = sbC("msC", [P, 2])
        rstdC = sbC("rstdC", [P, 2])
        mlp_stack.close()

        w_in_ld = sem("w_in_ld")
        small_ld = sem("small_ld")
        const_rdy = sem("const_rdy")
        setup_step = sem("setup_step")
        rot_setup = sem("rot_setup")
        turns_rdy = sem("turns_rdy")
        trig_rdy = sem("trig_rdy")
        x_ld = [sem("x_ld_even"), sem("x_ld_odd")]
        ss_rdy = sem("ss_rdy")
        ms_rdy = sem("ms_rdy")
        rstd_rdy = sem("rstd_rdy")
        xn_rdy = sem("xn_rdy")
        xT_ps = sem("xT_ps")
        hnT_rdy = sem("hnT_rdy")
        za_ps, zb_ps, zc_ps, zp_ps = sem("za_ps"), sem("zb_ps"), sem("zc_ps"), sem("zp_ps")
        za_ev, zb_ev, zc_ev, zp_ev = sem("za_ev"), sem("zb_ev"), sem("zc_ev"), sem("zp_ev")
        rot_step = sem("rot_step")
        qkT_ps = sem("qkT_ps")
        qT_ev = sem("qT_ev")
        kq_ev = sem("kq_ev")
        mixer_step = sem("mixer_step")
        edge_step = sem("edge_step")
        y_ps = sem("y_ps")
        y_ev = sem("y_ev")
        wo_ld = sem("wo_ld")
        q_ld = sem("q_ld")
        tail_ld = sem("tail_ld")
        idx_ps = sem("idx_ps")
        relu_rdy = sem("relu_rdy")
        score_step = sem("score_step")
        top_step = sem("top_step")
        mask_rdy = sem("mask_rdy")
        s_ps = sem("s_ps")
        masked_s = sem("masked_s")
        negmax_rdy = sem("negmax_rdy")
        exp_rdy = sem("exp_rdy")
        pT_ps = sem("pT_ps")
        pT_ev = sem("pT_ev")
        pv_ps = sem("pv_ps")
        invden_rdy = sem("invden_rdy")
        o_rdy = sem("o_rdy")
        oT_ps = sem("oT_ps")
        mixT_rdy = sem("mixT_rdy")
        wo_ps = sem("wo_ps")
        ssB_rdy = sem("ssB_rdy")
        msB_rdy = sem("msB_rdy")
        rstdB_rdy = sem("rstdB_rdy")
        h2_step = sem("h2_step")
        hn2_rdy = sem("hn2_rdy")
        hn2T_ps = sem("hn2T_ps")
        hn2T_rdy = sem("hn2T_rdy")
        h2_st = sem("h2_st")
        hn2T_st = sem("hn2T_st")
        wc_ld = sem("wc_ld")
        ring_ld = [sem(f"ring_ld{n}") for n in range(4)]
        ring_used = sem("ring_used")
        hn2T_ld = sem("hn2T_ld")
        h2_ld = sem("h2_ld")
        p_ld = sem("p_ld")
        pT2_ps = sem("pT2_ps")
        pT2_ev = sem("pT2_ev")
        up_ps = sem("up_ps")
        relu2_step = sem("relu2_step")
        hid_rdy = sem("hid_rdy")
        ssC_rdy = sem("ssC_rdy")
        msC_rdy = sem("msC_rdy")
        rstdC_rdy = sem("rstdC_rdy")
        m_step = sem("m_step")
        h3T_ps = sem("h3T_ps")
        h3T_rdy = sem("h3T_rdy")
        e_ps = sem("e_ps")
        gate_ps = sem("gate_ps")
        sig_rdy = sem("sig_rdy")
        ge_rdy = sem("ge_rdy")
        out_step = sem("out_step")
        out_st = sem("out_st")

        x_tiles = x[0].rearrange("(t p) d -> t p d", p=P)
        out_tiles = out[0].rearrange("(t p) d -> t p d", p=P)
        nblk = [len(blocks_of(g[2])) for g in GROUPS]
        picks = [g[0] * P >= KEEP for g in GROUPS]
        idx_n = Count([4 * n if s else 0 for n, s in zip(nblk, picks)])
        score_n = Count([4 * n + 1 if s else 0 for n, s in zip(nblk, picks)])
        top_n = Count([2 * KEEP // 8 + 1 if s else 0 for s in picks])
        head_n = Count([Q_HEADS * n for n in nblk])

        DOWN = ((0, 1, 2, 4), (5, 6, 3, 7))

        def split4(ap):
            return ap.rearrange("p (a b) -> p a b", b=P)

        def over(cols, width):
            return cols.unsqueeze(2).to_broadcast([P, cols.shape[1], width])

        block = ctx.enter_context(nc.Block())

        @block.sync
        def _(sp):
            def row_over_partitions(dst, src):
                return sp.dma_start(dst, src.to_broadcast([P, D]))

            sp.dma_start(pos_i[:], positions[0].rearrange("(t p) -> p t", p=P),
                         allow_slow_non_contiguous=True).then_inc(small_ld, 16)
            for dst, src in ((g_pre_col, g_mix_pre), (pool_scale_col, pool_scale), (g_mlp_col, g_mlp_pre)):
                sp.dma_start(dst[:], src[0].rearrange("(k p) -> p k", p=P),
                             allow_slow_non_contiguous=True).then_inc(small_ld, 16)
            sp.dma_start(w_pool_sb[:], w_pool[0].rearrange("g c d -> c g d")).then_inc(small_ld, 16)

            def load_x(i, u):
                sp.dma_start(x_in[:, u, :], x_tiles[i]).then_inc(x_ld[u], 16)

            load_x(0, 0)
            load_x(1, 1)
            for k in range(K):
                sp.dma_start(w_in_sb[:, k, :], w_in[0, k * P:(k + 1) * P, :]).then_inc(w_in_ld, 16)
            with sp.Fori(0, (T - 2) // 2) as ii:
                for u in range(2):
                    sp.wait_ge(xn_rdy, 2 * ii + u + 1)
                    sp.nop(nofuse=True)
                    load_x(2 * ii + u + 2, u)

            sp.wait_ge(y_ev, T)
            sp.nop(nofuse=True)
            sp.wait_ge(qT_ev, T)
            sp.nop(nofuse=True)
            sp.wait_ge(kq_ev, T)
            sp.nop(nofuse=True)
            sp.wait_ge(mixer_step, 10 * T)
            sp.nop(nofuse=True)
            for k in range(K):
                sp.dma_start(wo_sb[:, k, :], w_o[0, k * P:(k + 1) * P, :]).then_inc(wo_ld, 16)
            row_over_partitions(g_post_row[:], g_mix_post).then_inc(wo_ld, 16)

            def load_queries(g, t, i):
                sp.wait_ge(s_ps, head_n.at(g, t, 0))
                sp.nop(nofuse=True)
                sp.dma_start(qT_t[:], qT[:, :, bass.ts(i, P)]).then_inc(q_ld, 16)
                sp.dma_start(qiT_t[:], kq[:, 1:3, bass.ts(i, P)]).then_inc(q_ld, 16)

            def tail_traffic(i, first):
                if not first:
                    sp.wait_ge(wo_ps, i)
                    sp.nop(nofuse=True)
                    sp.wait_ge(h2_step, 3 * i)
                    sp.nop(nofuse=True)
                sp.dma_start(mixT_t[:, 4:8, :], poolT[:, :, bass.ts(i, P)]).then_inc(tail_ld, 16)
                sp.dma_start(x_t[:], x_tiles[i]).then_inc(tail_ld, 16)
                sp.wait_ge(h2_step, 3 * i + 3)
                sp.nop(nofuse=True)
                sp.dma_start(h2_dram[bass.ts(i, P), :], h2_t[:]).then_inc(h2_st, 16)
                sp.wait_ge(hn2T_rdy, 2 * i + 2)
                sp.nop(nofuse=True)
                sp.dma_start(hnT_dram[:, :, bass.ts(i, P)], hn2T_t[:]).then_inc(hn2T_st, 16)

            for g, (i0, n, keys) in enumerate(GROUPS):
                if g == 0:
                    load_queries(0, 0, 0)
                    load_queries(0, 1, 1)
                    tail_traffic(0, True)
                else:
                    with sp.Fori(0, n) as t:
                        load_queries(g, t, i0 + t)
                        tail_traffic(i0 + t - 1, False)
            tail_traffic(T - 1, False)

            sp.wait_ge(h2_st, 16 * T)
            sp.nop(nofuse=True)
            sp.wait_ge(hn2T_st, 16 * T)
            sp.nop(nofuse=True)
            for k in range(K):
                sp.dma_start(w_gate_sb[:, k, :], w_ple_gate[0, k * P:(k + 1) * P, :]).then_inc(wc_ld, 16)
            for k in range(KP):
                sp.dma_start(w_ple_sb[:, k, :], w_ple_proj[0, k * P:(k + 1) * P, :]).then_inc(wc_ld, 16)
            row_over_partitions(g_mlp_row[:], g_mlp_post).then_inc(wc_ld, 16)
            row_over_partitions(g_ple_row[:], g_ple_post).then_inc(wc_ld, 16)

            def chunk_traffic(c, first):
                if not first:
                    sp.wait_ge(up_ps, FT * c)
                    sp.nop(nofuse=True)
                    sp.wait_ge(pT2_ps, 2 * c)
                    sp.nop(nofuse=True)
                sp.dma_start(p_in[:], p[0, 0, bass.ts(c, CH), :].rearrange("(a q) d -> q a d", q=P)).then_inc(p_ld, 16)
                sp.dma_start(hn2T[:], hnT_dram[:, :, bass.ts(c, CH)]).then_inc(hn2T_ld, 16)
                for s in range(FT):
                    if 4 <= s < 20:
                        sp.wait_ge(up_ps, FT * c + 2 * (s - 4) + 2)
                        sp.nop(nofuse=True)
                    elif s >= 20:
                        sp.wait_ge(ring_used, 16 * c + s - 19)
                        sp.nop(nofuse=True)
                    elif not first:
                        sp.wait_ge(ring_used, 16 * c + s - 3)
                        sp.nop(nofuse=True)
                    dst = ring[:, s % 4, :]
                    if s < 16:
                        src = w_up[0, :, 256 * s:256 * (s + 1)].rearrange("(k q) f -> q k f", q=P)
                        dst = dst.rearrange("p (k f) -> p k f", f=256)
                    else:
                        half, q = (s - 16) // 8, (s - 16) % 8
                        src = w_down[0, 512 * q:512 * (q + 1), 512 * half:512 * (half + 1)].rearrange("(a q) d -> q a d", q=P)
                        dst = dst.rearrange("p (a d) -> p a d", d=512)
                    sp.dma_start(dst, src).then_inc(ring_ld[s % 4], 16)
                    if s == 8:
                        if not first:
                            sp.wait_ge(out_step, 2 * CT * c)
                            sp.nop(nofuse=True)
                        sp.dma_start(h2[:], h2_dram[bass.ts(c, CH), :].rearrange("(a q) d -> q a d", q=P)).then_inc(h2_ld, 16)

            chunk_traffic(0, True)
            with sp.Fori(1, NCH) as c:
                chunk_traffic(c, False)
            sp.wait_ge(out_st, 16 * T)
            sp.nop(nofuse=True)

        @block.gpsimd
        def _(pool):
            pool.memset(ident[:], 0.0).then_inc(setup_step, 1)
            pool.memset(causal[:], 0.0).then_inc(setup_step, 1)
            pool.memset(zp[:, :, 0:HALO], 0.0).then_inc(setup_step, 1)
            pool.memset(minus_half[:], -0.5).then_inc(setup_step, 1)
            for n in range(ROT_HALF):
                f = np.float32(THETA) ** np.float32(-2.0 * n / (2 * ROT_HALF))
                pool.memset(freq[:, n:n + 1], float(f)).then_inc(setup_step, 1)
            for g, w in enumerate(WINDOWS):
                pool.memset(edge[:, g, :], 1.0).then_inc(setup_step, 1)
            pool.wait_ge(setup_step, 4 + ROT_HALF + G)
            for g, w in enumerate(WINDOWS):
                for t in range(w - 1):
                    pool.memset(edge[:, g, t:t + 1], float(w) / (t + 1)).then_inc(const_rdy, 1)
            pool.affine_select(out=ident[:], in_=ident[:], compare_op=ALU.not_equal, fill=1.0, base=0,
                               pattern=[[-1, P]], channel_multiplier=1).then_inc(const_rdy, 1)
            pool.affine_select(out=causal[:], in_=causal[:], compare_op=ALU.is_ge, fill=MASKED, base=P,
                               pattern=[[-1, 384]], channel_multiplier=1).then_inc(const_rdy, 1)
            pool.wait_ge(const_rdy, sum(WINDOWS) - G + 2)

            def inv_root(i, u):
                pool.wait_ge(ms_rdy, i + 1)
                nc.gpsimd.tensor_tensor(rstd[:, u:u + 1], ms[:, u:u + 1], minus_half[:], ALU.pow).then_inc(rstd_rdy, 1)

            STEPS = 10

            def mixer(i, first):
                pool.wait_ge(zp_ev, i + 1)
                if not first:
                    pool.wait_ge(y_ps, i)
                W = HALO + P
                done = [0]

                def link(ins):
                    done[0] += 1
                    ins.then_inc(mixer_step, 1)
                    pool.wait_ge(mixer_step, i * STEPS + done[0])

                sums = [sum_a, sum_b, sum_a, sum_b]
                src = zp
                for g in range(G):
                    lo, sh = 2 ** (g + 1) - 1, 2 ** g
                    link(nc.gpsimd.tensor_tensor(sums[g][:, g:G, lo:W], src[:, g:G, lo:W],
                                                 src[:, g:G, lo - sh:W - sh], ALU.add))
                    src = sums[g]
                if first:
                    for g in range(G):
                        edged = sums[g][:, g, HALO:2 * HALO]
                        nc.gpsimd.tensor_tensor(edged, edged, edge[:, g, :], ALU.mult).then_inc(edge_step, 1)
                    pool.wait_ge(edge_step, G)
                for g, w in enumerate(WINDOWS):
                    pool.nop(nofuse=True)
                    link(nc.gpsimd.tensor_scalar(r_pool[:, g, :], sums[g][:, g, HALO:W], 1.0 / w, None, ALU.mult))
                link(nc.gpsimd.tensor_tensor(r_pool[:], r_pool[:], zp[:, :, HALO:W], ALU.subtract))
                pool.nop(nofuse=True)
                link(nc.gpsimd.tensor_copy(zp[:, :, 0:HALO], zp[:, :, P:P + HALO]))

            inv_root(0, 0)
            inv_root(1, 1)
            mixer(0, True)
            with pool.Fori(0, (T - 2) // 2) as ii:
                for u in range(2):
                    i = 2 * ii + u + 1
                    inv_root(i + 1, u)
                    mixer(i, False)
            mixer(T - 1, False)

            def tail_roots(i):
                for n in range(2):
                    pool.wait_ge(msB_rdy, 2 * i + n + 1)
                    nc.gpsimd.tensor_tensor(rstdB[:, n:n + 1], msB[:, n:n + 1], minus_half[:],
                                            ALU.pow).then_inc(rstdB_rdy, 1)

            with pool.Fori(0, T) as i:
                tail_roots(i)

            with pool.Fori(0, NCH) as c:
                for n in range(2 * CT):
                    col = n // CT
                    pool.wait_ge(msC_rdy, 2 * CT * c + n + 1)
                    nc.gpsimd.tensor_tensor(rstdC[:, col:col + 1], msC[:, col:col + 1], minus_half[:],
                                            ALU.pow).then_inc(rstdC_rdy, 1)

        @block.scalar
        def _(act):
            act.wait_ge(turns_rdy, 1)
            nc.scalar.activation(trig[:], turns[:], ACT.Sin).then_inc(trig_rdy, 1)

            def evacuate_z(i, u):
                zb = zs[:, u, :, :]
                act.wait_ge(za_ps, i + 1)
                nc.scalar.activation(zb[:, 0:8, :].rearrange("p (j g) d -> p g j d", g=2),
                                     bank[:, 2, :].rearrange("p (g j d) -> p g j d", g=2, d=HEAD),
                                     ACT.Copy, scale=HEAD ** -0.5).then_inc(za_ev, 1)
                act.wait_ge(zb_ps, i + 1)
                nc.scalar.copy(zb[:, 8:10, :], bank[:, 3, 0:128].rearrange("p (a d) -> p a d", d=HEAD)).then_inc(zb_ev, 1)
                nc.scalar.copy(values[:, i, :], bank[:, 3, 128:256]).then_inc(zb_ev, 1)
                nc.scalar.copy(zb[:, 10:14, :], bank[:, 3, 256:512].rearrange("p (a d) -> p a d", d=HEAD)).then_inc(zb_ev, 1)
                act.wait_ge(zc_ps, i + 1)
                nc.scalar.copy(zb[:, 14, :], bank[:, 4, 0:HEAD]).then_inc(zc_ev, 1)
                nc.scalar.activation(w_idx[:, i, :], bank[:, 4, HEAD:Z_C], ACT.Copy,
                                     scale=HEAD ** -0.5 * IDX_HEADS ** -0.5).then_inc(zc_ev, 1)

            def evacuate_pool(i, first):
                act.wait_ge(zp_ps, i + 1)
                if not first:
                    act.wait_ge(mixer_step, 10 * i)
                nc.scalar.copy(zp[:, :, HALO:], split4(bank[:, 5, :])).then_inc(zp_ev, 1)

            def evacuate_qT(i):
                act.wait_ge(qkT_ps, i + 1)
                nc.scalar.copy(qT[:, :, bass.ts(i, P)], split4(bank[:, 6, :])).then_inc(qT_ev, 1)

            act.wait_ge(setup_step, 4 + ROT_HALF + G)

            def step(i, u, x_round, first, last):
                if not first:
                    evacuate_qT(i - 1)
                if not last:
                    act.wait_ge(xT_ps, i + 1)
                    act.wait_ge(x_ld[1 - u], x_round)
                    nc.scalar.activation(xn[:], x_in[:, 1 - u, :], ACT.Square, scale=float(D) ** -0.5,
                                         accum_out=ss[:, 1 - u:2 - u]).then_inc(ss_rdy, 1)
                evacuate_z(i, u)
                evacuate_pool(i, first)

            act.wait_ge(x_ld[0], 16)
            nc.scalar.activation(xn[:], x_in[:, 0, :], ACT.Square, scale=float(D) ** -0.5,
                                 accum_out=ss[:, 0:1]).then_inc(ss_rdy, 1)
            step(0, 0, 16, True, False)
            with act.Fori(0, (T - 2) // 2) as ii:
                step(2 * ii + 1, 1, 16 * ii + 32, False, False)
                step(2 * ii + 2, 0, 16 * ii + 32, False, False)
            step(T - 1, 1, 0, False, True)
            evacuate_qT(T - 1)

            def idx_relu(g, t, n0, keys):
                n = 0
                for o, w in blocks_of(keys):
                    for h in range(IDX_HEADS):
                        act.wait_ge(idx_ps, idx_n.at(g, t, n + 1))
                        act.wait_ge(score_step, score_n.ring(g, t, n, 2))
                        nc.scalar.activation(relu[:, n % 2, 0:w], bank[:, n % 2, 0:w], ACT.Relu).then_inc(relu_rdy, 1)
                        n += 1

            def tail(i):
                act.wait_ge(oT_ps, i + 1)
                nc.scalar.copy(mixT_t[:, 0:4, :], split4(bank[:, 5, :])).then_inc(mixT_rdy, 1)
                for n in range(2):
                    act.wait_ge(wo_ps, i + 1)
                    nc.scalar.activation(hn2_t[:, n * 512:(n + 1) * 512], bank[:, n, :], ACT.Square,
                                         scale=float(D) ** -0.5, accum_out=ssB[:, n:n + 1]).then_inc(ssB_rdy, 1)
                act.wait_ge(h2_step, 3 * i + 3)
                nc.scalar.activation(hn2_t[:], h2_t[:], ACT.Square, scale=float(D) ** -0.5,
                                     accum_out=ssB[:, 2:3]).then_inc(ssB_rdy, 1)

            def attend(g, t, keys):
                blks = blocks_of(keys)
                nb = len(blks)

                def exp(h):
                    act.wait_ge(negmax_rdy, Q_HEADS * (GROUPS[g][0] + t) + h + 1)
                    nc.scalar.activation(probs[:, h % 2, 0:keys], probs[:, h % 2, 0:keys], ACT.Exp,
                                         bias=neg_max[:, h:h + 1], accum_out=denom[:, h:h + 1]).then_inc(exp_rdy, 1)

                exp(0)
                for h in range(Q_HEADS):
                    if h + 1 < Q_HEADS:
                        exp(h + 1)
                    for b, (o, w) in enumerate(blks):
                        m = h * nb + b
                        act.wait_ge(pT_ps, head_n.at(g, t, m + 1))
                        act.wait_ge(pv_ps, head_n.ring(g, t, m, 2))
                        nc.scalar.copy(probsT[:, m % 2, 0:w], bank[:, 5 + m % 2, 0:w]).then_inc(pT_ev, 1)

            def attn_step(g, t, i, keys, first):
                if picks[g]:
                    idx_relu(g, t, 0, keys)
                if not first:
                    tail(i - 1)
                attend(g, t, keys)

            for g, (i0, n, keys) in enumerate(GROUPS):
                if g == 0:
                    attn_step(0, 0, 0, keys, True)
                    attn_step(0, 1, 1, keys, False)
                else:
                    with act.Fori(0, n) as t:
                        attn_step(g, t, i0 + t, keys, False)
            tail(T - 1)

            def mlp_chunk(c):
                for n in range(2):
                    act.wait_ge(pT2_ps, 2 * c + n + 1)
                    nc.scalar.copy(pT[:, n, :], bank[:, (3, 7)[n], :]).then_inc(pT2_ev, 1)
                for f in range(FT):
                    act.wait_ge(up_ps, FT * c + f + 1)
                    nc.scalar.activation(hidden[:, f, :], bank[:, (3, 7)[f % 2], :], ACT.Relu).then_inc(relu2_step, 1)
                    act.wait_ge(relu2_step, FT * c + f + 1)
                    nc.scalar.activation(hidden[:, f, :], hidden[:, f, :], ACT.Square).then_inc(hid_rdy, 1)
                act.wait_ge(ring_used, FT // 2 * (c + 1))
                for a in range(CT):
                    for n in range(2):
                        nc.scalar.activation(junk[:, n * 512:(n + 1) * 512], bank[:, DOWN[n][a], :], ACT.Square,
                                             scale=float(D) ** -0.5, accum_out=ssC[:, n:n + 1]).then_inc(ssC_rdy, 1)
                    act.wait_ge(msC_rdy, 2 * CT * c + a + 1)
                for a in range(CT):
                    i = CT * c + a
                    act.wait_ge(out_step, 2 * i)
                    for n in range(2):
                        act.wait_ge(gate_ps, 2 * i + n + 1)
                        nc.scalar.activation(sig[:, n * 512:(n + 1) * 512], bank[:, (2, 4)[n], :],
                                             ACT.Sigmoid).then_inc(sig_rdy, 1)
                    for n in range(2):
                        act.wait_ge(ge_rdy, 2 * i + n + 1)
                        nc.scalar.activation(junk[:, n * 512:(n + 1) * 512], sig[:, n * 512:(n + 1) * 512], ACT.Square,
                                             scale=float(D) ** -0.5, accum_out=ssC[:, 2 + n:3 + n]).then_inc(ssC_rdy, 1)
                    act.wait_ge(out_step, 2 * i + 2)
                    act.dma_start(out[0, bass.ts(i, P), :], out_t[:]).then_inc(out_st, 16)

            with act.Fori(0, NCH) as c:
                mlp_chunk(c)

        @block.vector
        def _(dve):
            dve.wait_ge(small_ld, 16 * 5)
            dve.wait_ge(setup_step, 4 + ROT_HALF + G)
            done = [0]

            def link(ins):
                done[0] += 1
                ins.then_inc(rot_setup, 1)
                dve.wait_ge(rot_setup, done[0])

            link(nc.vector.tensor_copy(pos_f[:], pos_i[:]))
            link(nc.vector.tensor_tensor(angle[:], over(pos_f[:], ROT_HALF),
                                         freq[:].unsqueeze(1).to_broadcast([P, T, ROT_HALF]), ALU.mult))
            for n, (quarter, shift) in enumerate(((0.0, 0.0), (0.25, float(np.pi / 2)))):
                link(nc.vector.tensor_scalar(turns[:, n], angle[:], float(1 / (2 * np.pi)), quarter, ALU.mult, ALU.add))
                link(nc.vector.tensor_scalar(turns[:, n], turns[:, n], ROUND, None, ALU.add))
                link(nc.vector.tensor_scalar(turns[:, n], turns[:, n], -ROUND, None, ALU.add))
                rest = angle[:]
                for part in TWO_PI:
                    link(nc.vector.scalar_tensor_tensor(out=trig[:, n], in0=turns[:, n], scalar=float(-part), in1=rest,
                                                        op0=ALU.mult, op1=ALU.add))
                    rest = trig[:, n]
                link(nc.vector.tensor_scalar(turns[:, n], trig[:, n], shift, None, ALU.add))
                link(nc.vector.tensor_scalar(turns[:, n], turns[:, n], PI_SAFE, -PI_SAFE, ALU.min, ALU.max))
            nc.vector.tensor_copy(rot[:, 0, 0:1, 0:1], turns[:, 0, 0:1, 0:1]).then_inc(turns_rdy, 1)

            def norm(i, u):
                dve.wait_ge(ss_rdy, i + 1)
                nc.vector.tensor_scalar(ms[:, u:u + 1], ss[:, u:u + 1], EPS, None, ALU.add).then_inc(ms_rdy, 1)
                dve.wait_ge(rstd_rdy, i + 1)
                nc.vector.tensor_scalar(xn[:], x_in[:, u, :], rstd[:, u:u + 1], None, ALU.mult).then_inc(xn_rdy, 1)

            def evacuate_hnT(i):
                dve.wait_ge(xT_ps, i + 1)
                for n in range(2):
                    nc.vector.tensor_tensor(hnT[:, 4 * n:4 * n + 4, :], split4(bank[:, n, :]),
                                            over(g_pre_col[:, 4 * n:4 * n + 4], P), ALU.mult).then_inc(hnT_rdy, 1)

            def evacuate_kq(i):
                dve.wait_ge(qkT_ps, i + 1)
                nc.vector.tensor_copy(kq[:, :, bass.ts(i, P)], split4(bank[:, 7, :])).then_inc(kq_ev, 1)

            def evacuate_y(i):
                dve.wait_ge(y_ps, i + 1)
                nc.vector.tensor_tensor(poolT[:, :, bass.ts(i, P)], split4(bank[:, 0, :]),
                                        over(pool_scale_col[:], P), ALU.mult).then_inc(y_ev, 1)

            def rope(i, u):
                dve.wait_ge(za_ev, i + 1)
                dve.wait_ge(zb_ev, 3 * i + 3)
                dve.wait_ge(zc_ev, 2 * i + 2)
                zb = zs[:, u, 0:15, :]
                x1, x2 = zb[:, :, 0:ROT_HALF], zb[:, :, ROT_HALF:2 * ROT_HALF]
                sin, cos = (trig[:, n, i, :].unsqueeze(1).to_broadcast([P, 15, ROT_HALF]) for n in range(2))
                for n, (a, b) in enumerate(((x1, cos), (x2, sin), (x2, cos), (x1, sin))):
                    nc.vector.tensor_tensor(rot[:, n], a, b, ALU.mult).then_inc(rot_step, 1)
                dve.wait_ge(rot_step, 7 * i + 4)
                nc.vector.tensor_tensor(x1, rot[:, 0], rot[:, 1], ALU.subtract).then_inc(rot_step, 1)
                nc.vector.tensor_tensor(x2, rot[:, 2], rot[:, 3], ALU.add).then_inc(rot_step, 1)
                dve.wait_ge(rot_step, 7 * i + 6)
                nc.vector.tensor_copy(zs[:, u, 15, :], zs[:, u, 14, :]).then_inc(rot_step, 1)

            def step(i, u, first, last):
                evacuate_hnT(i)
                if not first:
                    evacuate_kq(i - 1)
                    evacuate_y(i - 1)
                if not last:
                    norm(i + 1, 1 - u)
                rope(i, u)

            norm(0, 0)
            dve.wait_ge(trig_rdy, 1)
            step(0, 0, True, False)
            with dve.Fori(0, (T - 2) // 2) as ii:
                step(2 * ii + 1, 1, False, False)
                step(2 * ii + 2, 0, False, False)
            step(T - 1, 1, False, True)
            evacuate_kq(T - 1)
            evacuate_y(T - 1)

            def weigh_scores(g, t, i, keys):
                n = 0
                for o, w in blocks_of(keys):
                    for h in range(IDX_HEADS):
                        dve.wait_ge(relu_rdy, idx_n.at(g, t, n + 1))
                        dst, wh = score[:, o:o + w], w_idx[:, i, h:h + 1]
                        if h == 0:
                            nc.vector.tensor_scalar(dst, relu[:, n % 2, 0:w], wh, None, ALU.mult).then_inc(score_step, 1)
                        else:
                            dve.wait_ge(score_step, score_n.at(g, t, n))
                            nc.vector.scalar_tensor_tensor(out=dst, in0=relu[:, n % 2, 0:w], scalar=wh, in1=dst,
                                                           op0=ALU.mult, op1=ALU.add).then_inc(score_step, 1)
                        n += 1
                dve.wait_ge(score_step, score_n.at(g, t, n))
                last = score[:, keys - 2 * P:keys]
                nc.vector.tensor_tensor(last, last, causal[:, bass.ds(P - P * t, 2 * P)], ALU.add).then_inc(score_step, 1)
                dve.wait_ge(score_step, score_n.at(g, t, n + 1))

            def take_top(g, t, keys, rounds):
                for r in rounds:
                    src = score if r == 0 else work
                    dve.nop(nofuse=True)
                    nc.vector.max(top8[:], src[:, 0:keys]).then_inc(top_step, 1)
                    dve.wait_ge(top_step, top_n.at(g, t, 2 * r + 1))
                    dve.nop(nofuse=True)
                    nc.vector.match_replace(work[:, 0:keys], top8[:], src[:, 0:keys], TAKEN).then_inc(top_step, 1)
                    dve.wait_ge(top_step, top_n.at(g, t, 2 * r + 2))

            def mask_rest(g, t, i, keys):
                nc.vector.tensor_tensor(work[:, 0:keys], work[:, 0:keys], score[:, 0:keys], ALU.is_equal).then_inc(top_step, 1)
                dve.wait_ge(top_step, top_n.at(g, t, KEEP // 4 + 1))
                nc.vector.tensor_scalar(work[:, 0:keys], work[:, 0:keys], MASKED, None, ALU.mult).then_inc(mask_rdy, 1)

            def residual(i):
                dve.wait_ge(ssB_rdy, 3 * i + 2)
                nc.vector.tensor_scalar(msB[:, 0:1], ssB[:, 0:1], ssB[:, 1:2], EPS, ALU.add, ALU.add).then_inc(msB_rdy, 1)
                dve.wait_ge(rstdB_rdy, 2 * i + 1)
                dve.wait_ge(h2_st, 16 * i)
                for n in range(2):
                    cols = slice(n * 512, (n + 1) * 512)
                    nc.vector.scalar_tensor_tensor(out=h2_t[:, cols], in0=bank[:, n, :], scalar=rstdB[:, 0:1],
                                                   in1=g_post_row[:, cols], op0=ALU.mult, op1=ALU.mult).then_inc(h2_step, 1)
                dve.wait_ge(h2_step, 3 * i + 2)
                dve.wait_ge(tail_ld, 32 * i + 32)
                nc.vector.tensor_tensor(h2_t[:], h2_t[:], x_t[:], ALU.add).then_inc(h2_step, 1)

            def normalise(i):
                dve.wait_ge(ssB_rdy, 3 * i + 3)
                nc.vector.tensor_scalar(msB[:, 1:2], ssB[:, 2:3], EPS, None, ALU.add).then_inc(msB_rdy, 1)
                dve.wait_ge(rstdB_rdy, 2 * i + 2)
                nc.vector.tensor_scalar(hn2_t[:], h2_t[:], rstdB[:, 1:2], None, ALU.mult).then_inc(hn2_rdy, 1)

            def evacuate_hn2T(i):
                dve.wait_ge(hn2T_ps, i + 1)
                dve.wait_ge(hn2T_st, 16 * i)
                for n in range(2):
                    nc.vector.tensor_tensor(hn2T_t[:, 4 * n:4 * n + 4, :], split4(bank[:, 5 + n, :]),
                                            over(g_mlp_col[:, 4 * n:4 * n + 4], P), ALU.mult).then_inc(hn2T_rdy, 1)

            def attend(g, t, i, keys):
                blks = blocks_of(keys)
                nb = len(blks)
                dve.wait_ge(mask_rdy, i + 1)
                for h in range(Q_HEADS):
                    dve.wait_ge(pT_ps, head_n.at(g, t, max(h - 1, 0) * nb))
                    for b, (o, w) in enumerate(blks):
                        m = h * nb + b
                        dve.wait_ge(s_ps, head_n.at(g, t, m + 1))
                        dve.nop(nofuse=True)
                        nc.vector.tensor_tensor_reduce(out=probs[:, h % 2, o:o + w], in0=bank[:, 2 + m % 3, 0:w],
                                                       in1=work[:, o:o + w], scale=1.0, scalar=TAKEN, op0=ALU.add,
                                                       op1=ALU.max, accum_out=block_max[:, h % 2, b:b + 1]).then_inc(masked_s, 1)
                    dve.wait_ge(masked_s, head_n.at(g, t, (h + 1) * nb))
                    nc.vector.tensor_reduce(neg_max[:, h:h + 1], block_max[:, h % 2, 0:nb], AX_X, ALU.max,
                                            negate=True).then_inc(negmax_rdy, 1)
                dve.wait_ge(pv_ps, head_n.at(g, t, Q_HEADS * nb))
                nc.vector.reciprocal(inv_denom[:], denom[:]).then_inc(invden_rdy, 1)
                dve.wait_ge(invden_rdy, i + 1)
                nc.vector.tensor_tensor(o_sb[:], bank[:, 7, :].rearrange("p (h d) -> p h d", d=HEAD),
                                        over(inv_denom[:], HEAD), ALU.mult).then_inc(o_rdy, 1)

            def attn_step(g, t, i, keys, first):
                rounds = range(KEEP // 8) if picks[g] else range(0)
                if picks[g]:
                    weigh_scores(g, t, i, keys)
                else:
                    nc.vector.tensor_copy(work[:, 0:keys], causal[:, P - P * t:3 * P - P * t]).then_inc(mask_rdy, 1)
                if not first:
                    residual(i - 1)
                take_top(g, t, keys, rounds[:8])
                if not first:
                    normalise(i - 1)
                take_top(g, t, keys, rounds[8:16])
                if not first:
                    evacuate_hn2T(i - 1)
                take_top(g, t, keys, rounds[16:])
                if picks[g]:
                    mask_rest(g, t, i, keys)
                attend(g, t, i, keys)

            dve.wait_ge(mixer_step, 10 * T)
            dve.wait_ge(const_rdy, sum(WINDOWS) - G + 2)
            dve.wait_ge(wo_ld, 16 * (K + 1))
            for g, (i0, n, keys) in enumerate(GROUPS):
                if g == 0:
                    attn_step(0, 0, 0, keys, True)
                    attn_step(0, 1, 1, keys, False)
                else:
                    with dve.Fori(0, n) as t:
                        attn_step(g, t, i0 + t, keys, False)
            residual(T - 1)
            normalise(T - 1)
            evacuate_hn2T(T - 1)

            dve.wait_ge(wc_ld, 16 * (K + KP + 2))

            def mlp_chunk(c):
                dve.wait_ge(h2_ld, 16 * c + 16)
                for a in range(CT):
                    i = CT * c + a
                    dve.wait_ge(ssC_rdy, 4 * CT * c + 2 * a + 2)
                    nc.vector.tensor_scalar(msC[:, 0:1], ssC[:, 0:1], ssC[:, 1:2], EPS, ALU.add, ALU.add).then_inc(msC_rdy, 1)
                    dve.wait_ge(rstdC_rdy, 2 * CT * c + a + 1)
                    for n in range(2):
                        cols = slice(n * 512, (n + 1) * 512)
                        nc.vector.scalar_tensor_tensor(out=m_t[:, cols], in0=bank[:, DOWN[n][a], :], scalar=rstdC[:, 0:1],
                                                       in1=g_mlp_row[:, cols], op0=ALU.mult, op1=ALU.mult).then_inc(m_step, 1)
                    dve.wait_ge(m_step, 3 * i + 2)
                    nc.vector.tensor_tensor(h2[:, a, :], h2[:, a, :], m_t[:], ALU.add).then_inc(m_step, 1)
                for a in range(CT):
                    i = CT * c + a
                    dve.wait_ge(h3T_ps, i + 1)
                    for n in range(2):
                        nc.vector.tensor_copy(h3T[:, 4 * n:4 * n + 4, :], split4(bank[:, (0, 5)[n], :])).then_inc(h3T_rdy, 1)
                    dve.wait_ge(e_ps, i + 1)
                    for n in range(2):
                        cols = slice(n * 512, (n + 1) * 512)
                        dve.wait_ge(sig_rdy, 2 * i + n + 1)
                        nc.vector.tensor_tensor(sig[:, cols], bank[:, (1, 6)[n], :], sig[:, cols], ALU.mult).then_inc(ge_rdy, 1)
                    dve.wait_ge(ssC_rdy, 4 * CT * c + 2 * CT + 2 * a + 2)
                    nc.vector.tensor_scalar(msC[:, 1:2], ssC[:, 2:3], ssC[:, 3:4], EPS, ALU.add, ALU.add).then_inc(msC_rdy, 1)
                    dve.wait_ge(rstdC_rdy, 2 * CT * c + CT + a + 1)
                    dve.wait_ge(out_st, 16 * i)
                    nc.vector.scalar_tensor_tensor(out=out_t[:], in0=sig[:], scalar=rstdC[:, 1:2], in1=g_ple_row[:],
                                                   op0=ALU.mult, op1=ALU.mult).then_inc(out_step, 1)
                    dve.wait_ge(out_step, 2 * i + 1)
                    nc.vector.tensor_tensor(out_t[:], out_t[:], h2[:, a, :], ALU.add).then_inc(out_step, 1)

            with dve.Fori(0, NCH) as c:
                mlp_chunk(c)

        @block.tensor
        def _(pe):
            pe.wait_ge(const_rdy, sum(WINDOWS) - G + 2)
            pe.wait_ge(small_ld, 16 * 5)

            def transposes(banks, src, done_sem):
                for n, b in enumerate(banks):
                    for a in range(4):
                        k = 4 * n + a
                        last = nc.tensor.transpose(bank[:, b, a * P:(a + 1) * P], src[:, k * P:(k + 1) * P], ident[:])
                last.then_inc(done_sem, 1)

            def transpose_x(i, first):
                pe.wait_ge(xn_rdy, i + 1)
                if not first:
                    pe.wait_ge(y_ev, i - 1)
                transposes((0, 1), xn, xT_ps)

            def transpose_qk(i, u):
                pe.wait_ge(rot_step, 7 * i + 7)
                pe.wait_ge(qT_ev, i)
                pe.wait_ge(kq_ev, i)
                transposes((6, 7), zs[:, u, :, :].rearrange("p a d -> p (a d)"), qkT_ps)

            def pool_product(i):
                pe.wait_ge(mixer_step, 10 * i + 9)
                for g in range(G):
                    last = nc.tensor.matmul(bank[:, 0, g * P:(g + 1) * P], w_pool_sb[:, g, :], r_pool[:, g, :],
                                            start=True, stop=True)
                last.then_inc(y_ps, 1)

            def project(i):
                for b, (lo, hi), ev, per, ps in ((2, (0, Z_A), za_ev, 1, za_ps), (3, (Z_A, Z_B), zb_ev, 3, zb_ps),
                                                 (4, (Z_B, Z_POOL), zc_ev, 2, zc_ps)):
                    pe.wait_ge(ev, per * i)
                    for k in range(K):
                        last = nc.tensor.matmul(bank[:, b, 0:hi - lo], hnT[:, k, :], w_in_sb[:, k, lo:hi],
                                                start=(k == 0), stop=(k == K - 1))
                    last.then_inc(ps, 1)
                pe.wait_ge(zp_ev, i)
                for g in range(G):
                    for k in range(K):
                        last = nc.tensor.matmul(bank[:, 5, g * P:(g + 1) * P],
                                                w_in_sb[:, k, Z_POOL + g * P:Z_POOL + (g + 1) * P], hnT[:, k, :],
                                                start=(k == 0), stop=(k == K - 1))
                last.then_inc(zp_ps, 1)

            def step(i, u, first):
                transpose_x(i, first)
                if not first:
                    transpose_qk(i - 1, 1 - u)
                pe.wait_ge(hnT_rdy, 2 * i + 2)
                if not first:
                    pool_product(i - 1)
                project(i)

            pe.wait_ge(w_in_ld, 16 * K)
            step(0, 0, True)
            with pe.Fori(0, (T - 2) // 2) as ii:
                step(2 * ii + 1, 1, False)
                step(2 * ii + 2, 0, False)
            step(T - 1, 1, False)
            transpose_qk(T - 1, 1)
            pool_product(T - 1)

            for s, n in ((za_ev, 1), (zb_ev, 3), (zc_ev, 2), (zp_ev, 1), (qT_ev, 1), (kq_ev, 1), (y_ev, 1), (mixer_step, 10)):
                pe.wait_ge(s, n * T)
            pe.wait_ge(wo_ld, 16 * (K + 1))

            def index(g, t, i, keys):
                pe.wait_ge(h2_step, 3 * (i - 1))
                n = 0
                for o, w in blocks_of(keys):
                    for h in range(IDX_HEADS):
                        j, lo = h // 2, HEAD * (h % 2)
                        pe.wait_ge(relu_rdy, idx_n.ring(g, t, n, 2))
                        nc.tensor.matmul(bank[:, n % 2, 0:w], qiT_t[lo:lo + HEAD, j, :], kq[lo:lo + HEAD, 3, o:o + w],
                                         start=True, stop=True).then_inc(idx_ps, 1)
                        n += 1
                pe.wait_ge(relu_rdy, idx_n.at(g, t, n))

            def output_projection(i):
                pe.wait_ge(o_rdy, i + 1)
                transposes((5,), o_sb[:].rearrange("p h d -> p (h d)"), oT_ps)
                pe.wait_ge(mixT_rdy, i + 1)
                pe.wait_ge(tail_ld, 32 * i + 32)
                for n in range(2):
                    for k in range(K):
                        last = nc.tensor.matmul(bank[:, n, :], mixT_t[:, k, :], wo_sb[:, k, n * 512:(n + 1) * 512],
                                                start=(k == 0), stop=(k == K - 1))
                last.then_inc(wo_ps, 1)

            def transpose_hn2(i):
                pe.wait_ge(hn2_rdy, i + 1)
                transposes((5, 6), hn2_t, hn2T_ps)
                pe.wait_ge(hn2T_rdy, 2 * i + 2)

            def attend(g, t, i, keys):
                blks = blocks_of(keys)
                nb = len(blks)

                def scores(h):
                    j, lo = h % 4, HEAD * (h // 4)
                    for b, (o, w) in enumerate(blks):
                        m = h * nb + b
                        pe.wait_ge(masked_s, head_n.ring(g, t, m, 3))
                        nc.tensor.matmul(bank[:, 2 + m % 3, 0:w], qT_t[lo:lo + HEAD, j, :], kq[lo:lo + HEAD, 0, o:o + w],
                                         start=True, stop=True).then_inc(s_ps, 1)

                def weigh(h, b):
                    o, w = blks[b]
                    m = h * nb + b
                    pe.wait_ge(pT_ev, head_n.at(g, t, m + 1))
                    for a in range(w // P):
                        kt = o // P + a
                        last = nc.tensor.matmul(bank[:, 7, h * HEAD:(h + 1) * HEAD], probsT[:, m % 2, a * P:(a + 1) * P],
                                                values[:, kt, HEAD * (h // 4):HEAD * (h // 4 + 1)],
                                                start=(kt == 0), stop=(kt == keys // P - 1))
                    last.then_inc(pv_ps, 1)

                pe.wait_ge(q_ld, 32 * i + 32)
                scores(0)
                for h in range(Q_HEADS):
                    if h + 1 < Q_HEADS:
                        scores(h + 1)
                    pe.wait_ge(exp_rdy, Q_HEADS * i + h + 1)
                    for b, (o, w) in enumerate(blks):
                        m = h * nb + b
                        pe.wait_ge(pT_ev, head_n.ring(g, t, m, 2))
                        for a in range(w // P):
                            last = nc.tensor.transpose(bank[:, 5 + m % 2, a * P:(a + 1) * P],
                                                       probs[:, h % 2, o + a * P:o + (a + 1) * P], ident[:])
                        last.then_inc(pT_ps, 1)
                        if b > 0:
                            weigh(h, b - 1)
                    weigh(h, nb - 1)

            def attn_step(g, t, i, keys, first):
                if picks[g]:
                    pe.wait_ge(q_ld, 32 * i + 32)
                    index(g, t, i, keys)
                if not first:
                    output_projection(i - 1)
                    transpose_hn2(i - 1)
                attend(g, t, i, keys)

            for g, (i0, n, keys) in enumerate(GROUPS):
                if g == 0:
                    attn_step(0, 0, 0, keys, True)
                    attn_step(0, 1, 1, keys, False)
                else:
                    with pe.Fori(0, n) as t:
                        attn_step(g, t, i0 + t, keys, False)
            output_projection(T - 1)
            transpose_hn2(T - 1)

            pe.wait_ge(wc_ld, 16 * (K + KP + 2))

            def mlp_chunk(c):
                pe.wait_ge(m_step, 3 * CT * c)
                pe.wait_ge(p_ld, 16 * c + 16)
                for k in range(KP):
                    for a in range(CT):
                        last = nc.tensor.transpose(bank[:, (3, 7)[k], a * P:(a + 1) * P], p_in[:, a, k * P:(k + 1) * P], ident[:])
                    last.then_inc(pT2_ps, 1)

                def weights(s):
                    pe.wait_ge(ring_ld[s % 4], 16 * (8 * c + s // 4 + 1))
                    return ring[:, s % 4, :]

                pe.wait_ge(hn2T_ld, 16 * c + 16)
                for f in range(FT):
                    if f % 2 == 0:
                        slot = weights(f // 2).rearrange("p (k f) -> p k f", f=256)
                    if f < 2:
                        pe.wait_ge(pT2_ev, 2 * c + f + 1)
                    else:
                        pe.wait_ge(relu2_step, FT * c + f - 1)
                    for k in range(K):
                        last = nc.tensor.matmul(bank[:, (3, 7)[f % 2], :], slot[:, k, (f % 2) * P:(f % 2 + 1) * P],
                                                hn2T[:, k, :], start=(k == 0), stop=(k == K - 1))
                    last.then_inc(up_ps, 1)

                pe.wait_ge(hid_rdy, FT * (c + 1))
                pe.wait_ge(h3T_rdy, 2 * CT * c)
                pe.wait_ge(ge_rdy, 2 * CT * c)
                pe.wait_ge(sig_rdy, 2 * CT * c)
                for half in range(2):
                    for q in range(8):
                        slot = weights(16 + 8 * half + q).rearrange("p (a d) -> p a d", d=512)
                        for r in range(4):
                            f = 4 * q + r
                            for a in range(CT):
                                last = nc.tensor.matmul(bank[:, DOWN[half][a], :], hidden[:, f, a * P:(a + 1) * P],
                                                        slot[:, r, :], start=(f == 0), stop=(f == FT - 1))
                        last.then_inc(ring_used, 1)

                for a in range(CT):
                    i = CT * c + a
                    pe.wait_ge(m_step, 3 * i + 3)
                    pe.wait_ge(h3T_rdy, 2 * i)
                    transposes((0, 5), h2[:, a, :], h3T_ps)
                    if a == 0:
                        pe.wait_ge(m_step, 3 * i + 6)
                    pe.wait_ge(ge_rdy, 2 * i)
                    for n in range(2):
                        for k in range(KP):
                            last = nc.tensor.matmul(bank[:, (1, 6)[n], :], pT[:, k, a * P:(a + 1) * P],
                                                    w_ple_sb[:, k, n * 512:(n + 1) * 512], start=(k == 0), stop=(k == KP - 1))
                    last.then_inc(e_ps, 1)
                    if a == 0:
                        pe.wait_ge(m_step, 3 * i + 12)
                    pe.wait_ge(h3T_rdy, 2 * i + 2)
                    pe.wait_ge(sig_rdy, 2 * i)
                    for n in range(2):
                        for k in range(K):
                            last = nc.tensor.matmul(bank[:, (2, 4)[n], :], h3T[:, k, :],
                                                    w_gate_sb[:, k, n * 512:(n + 1) * 512], start=(k == 0), stop=(k == K - 1))
                        last.then_inc(gate_ps, 1)

            with pe.Fori(0, NCH) as c:
                mlp_chunk(c)


_INS = ["x", "p", "positions", "g_mix_pre", "w_in", "w_pool", "pool_scale", "w_o", "g_mix_post",
        "g_mlp_pre", "w_up", "w_down", "g_mlp_post", "w_ple_gate", "w_ple_proj", "g_ple_post"]


def kernel(**inputs):
    import concourse.bacc as bacc
    from concourse.bass_utils import run_bass_kernel_spmd

    nc = bacc.Bacc("TRN2", target_bir_lowering=False, num_devices=1)
    arrays, args = {}, []
    for name in _INS:
        a = np.ascontiguousarray(inputs[name])
        arrays[f"in_{name}"] = a
        args.append(nc.dram_tensor(f"in_{name}", a.shape, mybir.dt.from_np(a.dtype), kind="ExternalInput").ap())
    shape = arrays["in_x"].shape
    args.append(nc.dram_tensor("out_h", shape, F32, kind="ExternalOutput").ap())
    hybrid_block(nc, *args)
    r = run_bass_kernel_spmd(nc, [arrays], core_ids=[0])
    return r.results[0]["out_h"]
```

```python
from contextlib import ExitStack

import numpy as np

import concourse.bass as bass
from concourse import mybir

P = 128
F32 = mybir.dt.float32
F32R = mybir.dt.float32r
I32 = mybir.dt.int32
ALU = mybir.AluOpType
ACT = mybir.ActivationFunctionType
AX_X = mybir.AxisListType.X

HEAD = 64
Q_HEADS = 8
KV_HEADS = 2
IDX_HEADS = 4
KEEP = 256
WINDOWS = (2, 4, 8, 16)
HALO = 16
ROT_HALF = 8
THETA = 500000.0
EPS = 1e-6
MASKED = -1.0e30
TAKEN = -3.0e38
ROUND = 12582912.0
TWO_PI = (6.28125, 1.9340515136718750e-3, 2 * np.pi - 6.28125 - 1.9340515136718750e-3)
PI_SAFE = 3.1415925

TILES = 16
STEPS = [(0, 1, P, 2 * P)] + [(i, 2, P * (i + 2), P * (i + 3)) for i in range(1, TILES - 1, 2)] + [(TILES - 1, 1, TILES * P, 0)]


def blocks_of(keys):
    tiles = keys // P
    n = -(-tiles // 4)
    cuts = [tiles * b // n * P for b in range(n + 1)]
    return [(lo, hi - lo) for lo, hi in zip(cuts, cuts[1:])]


class Count:

    def __init__(self, per_group):
        self.per = per_group
        self.before = [sum(per_group[g] * STEPS[g][1] for g in range(n)) for n in range(len(STEPS))]

    def at(self, g, t, k):
        return self.before[g] + t * self.per[g] + k


def hybrid_block(nc, x, p, positions, g_mix_pre, w_in, w_pool, pool_scale, w_o, g_mix_post,
                 g_mlp_pre, w_up, w_down, g_mlp_post, w_ple_gate, w_ple_proj, g_ple_post, out):
    S, D = x.shape[1], x.shape[2]
    T = S // P
    K = D // P
    W_IN = w_in.shape[2]
    FF = w_up.shape[2]
    PLE = p.shape[3]
    KP = PLE // P
    G = len(WINDOWS)
    Z_A, Z_B = 512, 1024
    Z_POOL = W_IN - G * P
    Z_C = Z_POOL - Z_B
    CH = 512
    CT = CH // P
    NCH = S // CH
    FT = FF // P
    ZB = Q_HEADS + IDX_HEADS + 2 * (KV_HEADS + 1)
    NQ = Q_HEADS + IDX_HEADS
    assert (S, D, T, K, FT) == (2048, 1024, 16, 8, 32) and Z_C == HEAD + IDX_HEADS

    h2_dram = nc.dram_tensor("h2_scratch", [S, D], F32, kind="Internal").ap()
    hnT_dram = nc.dram_tensor("hnT_scratch", [P, K, S], F32, kind="Internal").ap()
    q_dram = nc.dram_tensor("q_scratch", [S, NQ * HEAD], F32, kind="Internal").ap()
    pool_dram = nc.dram_tensor("pool_scratch", [P, G, S], F32, kind="Internal").ap()

    with ExitStack() as ctx:
        def alloc(stack):
            return lambda name, shape, dt=F32: stack.enter_context(nc.sbuf_tensor(name, shape, dt))

        def sem(name):
            return ctx.enter_context(nc.semaphore(name))

        bank = ctx.enter_context(nc.psum_tensor("bank", [P, 8, 512], F32))
        sb = alloc(ctx)
        ident = sb("ident", [P, P])
        minus_half = sb("minus_half", [P, 1])
        g_mlp_col = sb("g_mlp_col", [P, K])

        attn_stack = ExitStack()
        sbB0 = alloc(attn_stack)
        k_hi = sbB0("k_hi", [P, 3, S], F32R)
        k_lo = sbB0("k_lo", [P, 3, S], F32R)
        values = sbB0("values", [P, T, P])
        w_idx = sbB0("w_idx", [P, T, IDX_HEADS])
        causal = sbB0("causal", [P, 384])

        proj_stack = ExitStack()
        sbA = alloc(proj_stack)
        w_in_sb = sbA("w_in_sb", [P, K, W_IN])
        w_pool_sb = sbA("w_pool_sb", [P, G, P])
        g_pre_col = sbA("g_pre_col", [P, K])
        pool_scale_col = sbA("pool_scale_col", [P, G])
        x_in = sbA("x_in", [P, 2, D])
        xn = sbA("xn", [P, D])
        hnT = sbA("hnT", [P, K, P])
        zs = sbA("zs", [P, 2, ZB, HEAD])
        zp = sbA("zp", [P, G, HALO + P])
        sum_a = sbA("sum_a", [P, G, HALO + P])
        sum_b = sbA("sum_b", [P, G, HALO + P])
        edge = sbA("edge", [P, G, HALO])
        r_pool = sbA("r_pool", [P, G, P])
        y_pool = sbA("y_pool", [P, G, P])
        rot = sbA("rot", [P, 4, ZB, ROT_HALF])
        pos_i = sbA("pos_i", [P, T], I32)
        pos_f = sbA("pos_f", [P, T])
        freq = sbA("freq", [P, ROT_HALF])
        angle = sbA("angle", [P, T, ROT_HALF])
        turns = sbA("turns", [P, 2, T, ROT_HALF])
        trig = sbA("trig", [P, 2, T, ROT_HALF])
        ss = sbA("ss", [P, 2])
        ms = sbA("ms", [P, 2])
        rstd = sbA("rstd", [P, 2])
        proj_stack.close()

        tile_stack = ExitStack()
        sbB = alloc(tile_stack)
        wo_sb = sbB("wo_sb", [P, K, D])
        score = sbB("score", [P, S])
        work = sbB("work", [P, S])
        probs = sbB("probs", [P, 2, S])
        relu = sbB("relu", [P, 2, 512])
        probsT = sbB("probsT", [P, 2, 512])
        mask = sbB("mask", [P, S])
        q_t = sbB("q_t", [P, NQ, 2, HEAD])
        q_parts = sbB("q_parts", [P, NQ, P], F32R)
        mixT_t = sbB("mixT_t", [P, K, P])
        o_sb = sbB("o_sb", [P, Q_HEADS, HEAD])
        x_t = sbB("x_t", [P, D])
        h2_t = sbB("h2_t", [P, D])
        hn2_t = sbB("hn2_t", [P, D])
        hn2T_t = sbB("hn2T_t", [P, K, P])
        g_post_row = sbB("g_post_row", [P, D])
        top8 = sbB("top8", [P, 8])
        block_max = sbB("block_max", [P, 2, 4])
        neg_max = sbB("neg_max", [P, Q_HEADS])
        denom = sbB("denom", [P, Q_HEADS])
        inv_denom = sbB("inv_denom", [P, Q_HEADS])
        ssB = sbB("ssB", [P, 4])
        msB = sbB("msB", [P, 2])
        rstdB = sbB("rstdB", [P, 2])
        tile_stack.close()
        attn_stack.close()

        mlp_stack = ExitStack()
        sbC = alloc(mlp_stack)
        ring = sbC("ring", [P, 4, 2048])
        hidden = sbC("hidden", [P, FT, CH])
        hn2T = sbC("hn2T", [P, K, CH])
        h2 = sbC("h2", [P, CT, D])
        w_gate_sb = sbC("w_gate_sb", [P, K, D])
        w_ple_sb = sbC("w_ple_sb", [P, KP, D])
        g_mlp_row = sbC("g_mlp_row", [P, D])
        g_ple_row = sbC("g_ple_row", [P, D])
        p_in = sbC("p_in", [P, CT, PLE])
        pT = sbC("pT", [P, KP, CH])
        m_t = sbC("m_t", [P, D])
        h3T = sbC("h3T", [P, K, P])
        sig = sbC("sig", [P, D])
        out_t = sbC("out_t", [P, D])
        junk = sbC("junk", [P, D])
        ssC = sbC("ssC", [P, 4])
        msC = sbC("msC", [P, 2])
        rstdC = sbC("rstdC", [P, 2])
        mlp_stack.close()

        w_in_ld = sem("w_in_ld")
        small_ld = sem("small_ld")
        const_rdy = sem("const_rdy")
        setup_step = sem("setup_step")
        rot_setup = sem("rot_setup")
        turns_rdy = sem("turns_rdy")
        trig_rdy = sem("trig_rdy")
        x_ld = [sem("x_ld_even"), sem("x_ld_odd")]
        ss_rdy = sem("ss_rdy")
        ms_rdy = sem("ms_rdy")
        rstd_rdy = sem("rstd_rdy")
        xn_rdy = sem("xn_rdy")
        xT_ps = sem("xT_ps")
        hnT_rdy = sem("hnT_rdy")
        za_ps, zb_ps, zc_ps, zp_ps = sem("za_ps"), sem("zb_ps"), sem("zc_ps"), sem("zp_ps")
        za_ev, zb_ev, zc_ev, zp_ev = sem("za_ev"), sem("zb_ev"), sem("zc_ev"), sem("zp_ev")
        rot_step = sem("rot_step")
        kT_ps = sem("kT_ps")
        k_hi_ev = sem("k_hi_ev")
        k_lo_ev = sem("k_lo_ev")
        q_st = [sem("q_st_even"), sem("q_st_odd")]
        pool_st = sem("pool_st")
        mixer_step = sem("mixer_step")
        edge_step = sem("edge_step")
        y_ps = sem("y_ps")
        y_ev = sem("y_ev")
        wo_ld = sem("wo_ld")
        q_ld = sem("q_ld")
        qi_ld = sem("qi_ld")
        qT_ps = sem("qT_ps")
        q_hi = sem("q_hi")
        q_lo = sem("q_lo")
        qiT_ps = sem("qiT_ps")
        qi_hi = sem("qi_hi")
        qi_lo = sem("qi_lo")
        tail_ld = sem("tail_ld")
        idx_ps = sem("idx_ps")
        relu_rdy = sem("relu_rdy")
        score_step = sem("score_step")
        top_step = sem("top_step")
        mask_rdy = sem("mask_rdy")
        s_ps = sem("s_ps")
        masked_s = sem("masked_s")
        negmax_rdy = sem("negmax_rdy")
        exp_rdy = sem("exp_rdy")
        pT_ps = sem("pT_ps")
        pT_ev = sem("pT_ev")
        pv_ps = sem("pv_ps")
        invden_rdy = sem("invden_rdy")
        o_rdy = sem("o_rdy")
        oT_ps = sem("oT_ps")
        mixT_rdy = sem("mixT_rdy")
        wo_ps = sem("wo_ps")
        ssB_rdy = sem("ssB_rdy")
        msB_rdy = sem("msB_rdy")
        rstdB_rdy = sem("rstdB_rdy")
        h2_step = sem("h2_step")
        hn2_rdy = sem("hn2_rdy")
        hn2T_ps = sem("hn2T_ps")
        hn2T_rdy = sem("hn2T_rdy")
        h2_st = sem("h2_st")
        hn2T_st = sem("hn2T_st")
        wc_ld = sem("wc_ld")
        ring_ld = [sem(f"ring_ld{n}") for n in range(4)]
        ring_used = sem("ring_used")
        hn2T_ld = sem("hn2T_ld")
        h2_ld = sem("h2_ld")
        p_ld = sem("p_ld")
        pT2_ps = sem("pT2_ps")
        pT2_ev = sem("pT2_ev")
        up_ps = sem("up_ps")
        relu2_step = sem("relu2_step")
        hid_rdy = sem("hid_rdy")
        ssC_rdy = sem("ssC_rdy")
        msC_rdy = sem("msC_rdy")
        rstdC_rdy = sem("rstdC_rdy")
        m_step = sem("m_step")
        h3T_ps = sem("h3T_ps")
        h3T_rdy = sem("h3T_rdy")
        e_ps = sem("e_ps")
        gate_ps = sem("gate_ps")
        sig_rdy = sem("sig_rdy")
        ge_rdy = sem("ge_rdy")
        out_step = sem("out_step")
        out_st = sem("out_st")

        x_tiles = x[0].rearrange("(t p) d -> t p d", p=P)
        out_tiles = out[0].rearrange("(t p) d -> t p d", p=P)
        top_blocks = [len(blocks_of(g[3])) if g[3] > KEEP else 0 for g in STEPS]
        idx_n = Count([IDX_HEADS * n for n in top_blocks])
        score_n = Count([IDX_HEADS * n + 1 if n else 0 for n in top_blocks])
        top_n = Count([2 * KEEP // 8 + 1 if n else 0 for n in top_blocks])
        head_n = Count([Q_HEADS * len(blocks_of(g[2])) for g in STEPS])

        DOWN = ((0, 1, 2, 4), (5, 6, 3, 7))

        def split4(ap):
            return ap.rearrange("p (a b) -> p a b", b=P)

        def over(cols, width):
            return cols.unsqueeze(2).to_broadcast([P, cols.shape[1], width])

        def twice(ap):
            heads = ap.rearrange("p (a d) -> p a d", d=HEAD)
            return heads.unsqueeze(2).to_broadcast([P, heads.shape[1], 2, HEAD])

        block = ctx.enter_context(nc.Block())

        @block.sync
        def _(sp):
            def row_over_partitions(dst, src):
                return sp.dma_start(dst, src.to_broadcast([P, D]))

            sp.dma_start(pos_i[:], positions[0].rearrange("(t p) -> p t", p=P),
                         allow_slow_non_contiguous=True).then_inc(small_ld, 16)
            for dst, src in ((g_pre_col, g_mix_pre), (pool_scale_col, pool_scale), (g_mlp_col, g_mlp_pre)):
                sp.dma_start(dst[:], src[0].rearrange("(k p) -> p k", p=P),
                             allow_slow_non_contiguous=True).then_inc(small_ld, 16)
            sp.dma_start(w_pool_sb[:], w_pool[0].rearrange("g c d -> c g d")).then_inc(small_ld, 16)

            def load_x(i, u):
                sp.dma_start(x_in[:, u, :], x_tiles[i]).then_inc(x_ld[u], 16)

            def hold():
                sp.nop(nofuse=True)

            load_x(0, 0)
            load_x(1, 1)
            for k in range(K):
                sp.dma_start(w_in_sb[:, k, :], w_in[0, k * P:(k + 1) * P, :]).then_inc(w_in_ld, 16)

            def projection_traffic(i, u, last):
                sp.wait_ge(xn_rdy, i + 1)
                hold()
                if not last:
                    load_x(i + 2, u)
                sp.wait_ge(rot_step, 6 * i + 6)
                hold()
                sp.dma_start(q_dram[bass.ts(i, P), :], zs[:, u, 0:NQ, :].rearrange("p a d -> p (a d)")).then_inc(q_st[u], 16)
                sp.wait_ge(y_ev, i + 1)
                hold()
                sp.dma_start(pool_dram[:, :, bass.ts(i, P)], y_pool[:]).then_inc(pool_st, 16)

            projection_traffic(0, 0, False)
            projection_traffic(1, 1, False)
            with sp.Fori(0, (T - 4) // 2) as ii:
                projection_traffic(2 * ii + 2, 0, False)
                projection_traffic(2 * ii + 3, 1, False)
            projection_traffic(T - 2, 0, True)
            projection_traffic(T - 1, 1, True)

            sp.wait_ge(k_hi_ev, T)
            sp.wait_ge(k_lo_ev, T)
            sp.wait_ge(mixer_step, 10 * T)
            sp.wait_ge(q_st[0], 8 * T)
            sp.wait_ge(q_st[1], 8 * T)
            sp.wait_ge(pool_st, 16 * T)
            for k in range(K):
                sp.dma_start(wo_sb[:, k, :], w_o[0, k * P:(k + 1) * P, :]).then_inc(wo_ld, 16)
            row_over_partitions(g_post_row[:], g_mix_post).then_inc(wo_ld, 16)

            def tail_traffic(i, first):
                if not first:
                    sp.wait_ge(wo_ps, i)
                    hold()
                sp.dma_start(mixT_t[:, 4:8, :], pool_dram[:, :, bass.ts(i, P)]).then_inc(tail_ld, 16)
                if not first:
                    sp.wait_ge(h2_step, 3 * i)
                    hold()
                sp.dma_start(x_t[:], x_tiles[i]).then_inc(tail_ld, 16)
                sp.wait_ge(h2_step, 3 * i + 3)
                hold()
                sp.dma_start(h2_dram[bass.ts(i, P), :], h2_t[:]).then_inc(h2_st, 16)
                sp.wait_ge(hn2T_rdy, 2 * i + 2)
                hold()
                sp.dma_start(hnT_dram[:, :, bass.ts(i, P)], hn2T_t[:]).then_inc(hn2T_st, 16)

            def step_traffic(i, g, first, first_tail=False):
                if not first:
                    sp.wait_ge(qT_ps, i)
                    hold()
                for e in range(2):
                    heads = q_dram[bass.ts(i, P), 0:Q_HEADS * HEAD].rearrange("p (a d) -> p a d", d=HEAD)
                    sp.dma_start(q_t[:, 0:Q_HEADS, e, :], heads).then_inc(q_ld, 16)
                if top_blocks[g]:
                    for e in range(2):
                        heads = q_dram[bass.ds(P * i + P, P), Q_HEADS * HEAD:].rearrange("p (a d) -> p a d", d=HEAD)
                        sp.dma_start(q_t[:, Q_HEADS:, e, :], heads).then_inc(qi_ld, 16)
                if not first:
                    tail_traffic(i - 1, first_tail)

            step_traffic(0, 0, True)
            for g in range(1, len(STEPS) - 1):
                i0, n = STEPS[g][:2]
                if g == 1:
                    step_traffic(1, 1, False, True)
                    step_traffic(2, 1, False)
                else:
                    with sp.Fori(0, n) as t:
                        step_traffic(i0 + t, g, False)
            step_traffic(T - 1, len(STEPS) - 1, False)
            tail_traffic(T - 1, False)

            sp.wait_ge(h2_st, 16 * T)
            sp.nop(nofuse=True)
            sp.wait_ge(hn2T_st, 16 * T)
            sp.nop(nofuse=True)
            for k in range(K):
                sp.dma_start(w_gate_sb[:, k, :], w_ple_gate[0, k * P:(k + 1) * P, :]).then_inc(wc_ld, 16)
            for k in range(KP):
                sp.dma_start(w_ple_sb[:, k, :], w_ple_proj[0, k * P:(k + 1) * P, :]).then_inc(wc_ld, 16)
            row_over_partitions(g_mlp_row[:], g_mlp_post).then_inc(wc_ld, 16)
            row_over_partitions(g_ple_row[:], g_ple_post).then_inc(wc_ld, 16)

            def chunk_traffic(c, first):
                if not first:
                    sp.wait_ge(up_ps, FT * c)
                    sp.nop(nofuse=True)
                    sp.wait_ge(pT2_ps, 2 * c)
                    sp.nop(nofuse=True)
                sp.dma_start(p_in[:], p[0, 0, bass.ts(c, CH), :].rearrange("(a q) d -> q a d", q=P)).then_inc(p_ld, 16)
                sp.dma_start(hn2T[:], hnT_dram[:, :, bass.ts(c, CH)]).then_inc(hn2T_ld, 16)
                for s in range(FT):
                    if 4 <= s < 20:
                        sp.wait_ge(up_ps, FT * c + 2 * (s - 4) + 2)
                        sp.nop(nofuse=True)
                    elif s >= 20:
                        sp.wait_ge(ring_used, 16 * c + s - 19)
                        sp.nop(nofuse=True)
                    elif not first:
                        sp.wait_ge(ring_used, 16 * c + s - 3)
                        sp.nop(nofuse=True)
                    dst = ring[:, s % 4, :]
                    if s < 16:
                        src = w_up[0, :, 256 * s:256 * (s + 1)].rearrange("(k q) f -> q k f", q=P)
                        dst = dst.rearrange("p (k f) -> p k f", f=256)
                    else:
                        half, q = (s - 16) // 8, (s - 16) % 8
                        src = w_down[0, 512 * q:512 * (q + 1), 512 * half:512 * (half + 1)].rearrange("(a q) d -> q a d", q=P)
                        dst = dst.rearrange("p (a d) -> p a d", d=512)
                    sp.dma_start(dst, src).then_inc(ring_ld[s % 4], 16)
                    if s == 8:
                        if not first:
                            sp.wait_ge(out_step, 2 * CT * c)
                            sp.nop(nofuse=True)
                        sp.dma_start(h2[:], h2_dram[bass.ts(c, CH), :].rearrange("(a q) d -> q a d", q=P)).then_inc(h2_ld, 16)

            chunk_traffic(0, True)
            with sp.Fori(1, NCH) as c:
                chunk_traffic(c, False)
            sp.wait_ge(out_st, 16 * T)
            sp.nop(nofuse=True)

        @block.gpsimd
        def _(pool):
            pool.memset(ident[:], 0.0).then_inc(setup_step, 1)
            pool.memset(causal[:], 0.0).then_inc(setup_step, 1)
            pool.memset(zp[:, :, 0:HALO], 0.0).then_inc(setup_step, 1)
            pool.memset(minus_half[:], -0.5).then_inc(setup_step, 1)
            for n in range(ROT_HALF):
                f = np.float32(THETA) ** np.float32(-2.0 * n / (2 * ROT_HALF))
                pool.memset(freq[:, n:n + 1], float(f)).then_inc(setup_step, 1)
            for g, w in enumerate(WINDOWS):
                pool.memset(edge[:, g, :], 1.0).then_inc(setup_step, 1)
            pool.wait_ge(setup_step, 4 + ROT_HALF + G)
            for g, w in enumerate(WINDOWS):
                for t in range(w - 1):
                    pool.memset(edge[:, g, t:t + 1], float(w) / (t + 1)).then_inc(const_rdy, 1)
            pool.affine_select(out=ident[:], in_=ident[:], compare_op=ALU.not_equal, fill=1.0, base=0,
                               pattern=[[-1, P]], channel_multiplier=1).then_inc(const_rdy, 1)
            pool.affine_select(out=causal[:], in_=causal[:], compare_op=ALU.is_ge, fill=MASKED, base=P,
                               pattern=[[-1, 384]], channel_multiplier=1).then_inc(const_rdy, 1)
            pool.wait_ge(const_rdy, sum(WINDOWS) - G + 2)

            def inv_root(i, u):
                pool.wait_ge(ms_rdy, i + 1)
                nc.gpsimd.tensor_tensor(rstd[:, u:u + 1], ms[:, u:u + 1], minus_half[:], ALU.pow).then_inc(rstd_rdy, 1)

            STEPS = 10

            def mixer(i, first):
                pool.wait_ge(zp_ev, i + 1)
                if not first:
                    pool.wait_ge(y_ps, i)
                W = HALO + P
                done = [0]

                def link(ins):
                    done[0] += 1
                    ins.then_inc(mixer_step, 1)
                    pool.wait_ge(mixer_step, i * STEPS + done[0])

                sums = [sum_a, sum_b, sum_a, sum_b]
                src = zp
                for g in range(G):
                    lo, sh = 2 ** (g + 1) - 1, 2 ** g
                    link(nc.gpsimd.tensor_tensor(sums[g][:, g:G, lo:W], src[:, g:G, lo:W],
                                                 src[:, g:G, lo - sh:W - sh], ALU.add))
                    src = sums[g]
                if first:
                    for g in range(G):
                        edged = sums[g][:, g, HALO:2 * HALO]
                        nc.gpsimd.tensor_tensor(edged, edged, edge[:, g, :], ALU.mult).then_inc(edge_step, 1)
                    pool.wait_ge(edge_step, G)
                for g, w in enumerate(WINDOWS):
                    pool.nop(nofuse=True)
                    link(nc.gpsimd.tensor_scalar(r_pool[:, g, :], sums[g][:, g, HALO:W], 1.0 / w, None, ALU.mult))
                link(nc.gpsimd.tensor_tensor(r_pool[:], r_pool[:], zp[:, :, HALO:W], ALU.subtract))
                pool.nop(nofuse=True)
                link(nc.gpsimd.tensor_copy(zp[:, :, 0:HALO], zp[:, :, P:P + HALO]))

            inv_root(0, 0)
            inv_root(1, 1)
            mixer(0, True)
            inv_root(2, 0)
            mixer(1, False)
            with pool.Fori(0, (T - 4) // 2) as ii:
                for u in range(2):
                    inv_root(2 * ii + 3 + u, 1 - u)
                    mixer(2 * ii + 2 + u, False)
            inv_root(T - 1, 1)
            mixer(T - 2, False)
            mixer(T - 1, False)

            def tail_roots(i):
                for n in range(2):
                    pool.wait_ge(msB_rdy, 2 * i + n + 1)
                    nc.gpsimd.tensor_tensor(rstdB[:, n:n + 1], msB[:, n:n + 1], minus_half[:],
                                            ALU.pow).then_inc(rstdB_rdy, 1)

            with pool.Fori(0, T) as i:
                tail_roots(i)

            with pool.Fori(0, NCH) as c:
                for n in range(2 * CT):
                    col = n // CT
                    pool.wait_ge(msC_rdy, 2 * CT * c + n + 1)
                    nc.gpsimd.tensor_tensor(rstdC[:, col:col + 1], msC[:, col:col + 1], minus_half[:],
                                            ALU.pow).then_inc(rstdC_rdy, 1)

        @block.scalar
        def _(act):
            act.wait_ge(turns_rdy, 1)
            nc.scalar.activation(trig[:], turns[:], ACT.Sin).then_inc(trig_rdy, 1)

            def evacuate_z(i, u, stored):
                zb = zs[:, u, :, :]
                if stored is not None:
                    act.wait_ge(q_st[u], stored)
                act.wait_ge(za_ps, i + 1)
                nc.scalar.activation(zb[:, 0:8, :], bank[:, 2, :].rearrange("p (a d) -> p a d", d=HEAD),
                                     ACT.Copy, scale=HEAD ** -0.5).then_inc(za_ev, 1)
                act.wait_ge(zb_ps, i + 1)
                nc.scalar.copy(zb[:, 12:16, :].rearrange("p (a e) d -> p a e d", e=2), twice(bank[:, 3, 0:128])).then_inc(zb_ev, 1)
                nc.scalar.copy(values[:, i, :], bank[:, 3, 128:256]).then_inc(zb_ev, 1)
                nc.scalar.copy(zb[:, 8:12, :], bank[:, 3, 256:512].rearrange("p (a d) -> p a d", d=HEAD)).then_inc(zb_ev, 1)
                act.wait_ge(zc_ps, i + 1)
                nc.scalar.copy(zb[:, 16:18, :].rearrange("p (a e) d -> p a e d", e=2), twice(bank[:, 4, 0:HEAD])).then_inc(zc_ev, 1)
                nc.scalar.activation(w_idx[:, i, :], bank[:, 4, HEAD:Z_C], ACT.Copy,
                                     scale=HEAD ** -0.5 * IDX_HEADS ** -0.5).then_inc(zc_ev, 1)

            def evacuate_pool(i, first):
                act.wait_ge(zp_ps, i + 1)
                if not first:
                    act.wait_ge(mixer_step, 10 * i)
                nc.scalar.copy(zp[:, :, HALO:], split4(bank[:, 5, :])).then_inc(zp_ev, 1)

            def evacuate_k(i):
                act.wait_ge(kT_ps, i + 1)
                nc.scalar.copy(k_hi[:, :, bass.ts(i, P)], split4(bank[:, 6, 0:3 * P])).then_inc(k_hi_ev, 1)

            act.wait_ge(setup_step, 4 + ROT_HALF + G)

            def step(i, u, x_round, stored, first=False, last=False):
                if not first:
                    evacuate_k(i - 1)
                if not last:
                    act.wait_ge(xT_ps, i + 1)
                    act.wait_ge(x_ld[1 - u], x_round)
                    nc.scalar.activation(xn[:], x_in[:, 1 - u, :], ACT.Square, scale=float(D) ** -0.5,
                                         accum_out=ss[:, 1 - u:2 - u]).then_inc(ss_rdy, 1)
                evacuate_z(i, u, stored)
                evacuate_pool(i, first)

            act.wait_ge(x_ld[0], 16)
            nc.scalar.activation(xn[:], x_in[:, 0, :], ACT.Square, scale=float(D) ** -0.5,
                                 accum_out=ss[:, 0:1]).then_inc(ss_rdy, 1)
            step(0, 0, 16, None, first=True)
            step(1, 1, 32, None)
            with act.Fori(0, (T - 4) // 2) as ii:
                step(2 * ii + 2, 0, 16 * ii + 32, 16 * ii + 16)
                step(2 * ii + 3, 1, 16 * ii + 48, 16 * ii + 16)
            step(T - 2, 0, 8 * T, 8 * T - 16)
            step(T - 1, 1, None, 8 * T - 16, last=True)
            evacuate_k(T - 1)

            def split_queries(i, indexer):
                if indexer:
                    act.wait_ge(qiT_ps, i)
                    nc.scalar.copy(q_parts[:, Q_HEADS:, :], split4(bank[:, 2, :])).then_inc(qi_hi, 1)
                act.wait_ge(qT_ps, i + 1)
                for n in range(2):
                    nc.scalar.copy(q_parts[:, 4 * n:4 * n + 4, :], split4(bank[:, 5 + n, :])).then_inc(q_hi, 1)

            def idx_relu(g, t):
                n = 0
                for o, w in blocks_of(STEPS[g][3]):
                    for h in range(IDX_HEADS):
                        act.wait_ge(idx_ps, idx_n.at(g, t, n + 1))
                        if n >= 2:
                            act.wait_ge(score_step, score_n.at(g, t, n - 1))
                        nc.scalar.activation(relu[:, n % 2, 0:w], bank[:, n % 2, 0:w], ACT.Relu).then_inc(relu_rdy, 1)
                        n += 1

            def tail(i):
                act.wait_ge(oT_ps, i + 1)
                nc.scalar.copy(mixT_t[:, 0:4, :], split4(bank[:, 5, :])).then_inc(mixT_rdy, 1)
                for n in range(2):
                    act.wait_ge(wo_ps, i + 1)
                    nc.scalar.activation(hn2_t[:, n * 512:(n + 1) * 512], bank[:, n, :], ACT.Square,
                                         scale=float(D) ** -0.5, accum_out=ssB[:, n:n + 1]).then_inc(ssB_rdy, 1)
                act.wait_ge(h2_step, 3 * i + 3)
                nc.scalar.activation(hn2_t[:], h2_t[:], ACT.Square, scale=float(D) ** -0.5,
                                     accum_out=ssB[:, 2:3]).then_inc(ssB_rdy, 1)

            def attend(g, t, i):
                keys = STEPS[g][2]
                blks = blocks_of(keys)
                nb = len(blks)

                def exp(h):
                    act.wait_ge(negmax_rdy, Q_HEADS * i + h + 1)
                    nc.scalar.activation(probs[:, h % 2, 0:keys], probs[:, h % 2, 0:keys], ACT.Exp,
                                         bias=neg_max[:, h:h + 1], accum_out=denom[:, h:h + 1]).then_inc(exp_rdy, 1)

                exp(0)
                for h in range(Q_HEADS):
                    if h + 1 < Q_HEADS:
                        exp(h + 1)
                    for b, (o, w) in enumerate(blks):
                        m = h * nb + b
                        act.wait_ge(pT_ps, head_n.at(g, t, m + 1))
                        if m >= 2:
                            act.wait_ge(pv_ps, head_n.at(g, t, m - 1))
                        nc.scalar.copy(probsT[:, m % 2, 0:w], bank[:, 5 + m % 2, 0:w]).then_inc(pT_ev, 1)

            def attn_step(g, t, i):
                split_queries(i, top_blocks[g] > 0)
                if top_blocks[g]:
                    idx_relu(g, t)
                if g > 0:
                    tail(i - 1)
                attend(g, t, i)

            for g, (i0, n, _, _) in enumerate(STEPS):
                if g < 2 or n == 1:
                    for t in range(n):
                        attn_step(g, t, i0 + t)
                else:
                    with act.Fori(0, n) as t:
                        attn_step(g, t, i0 + t)
            tail(T - 1)

            def mlp_chunk(c, first):
                for n in range(2):
                    act.wait_ge(pT2_ps, 2 * c + n + 1)
                    nc.scalar.copy(pT[:, n, :], bank[:, (3, 7)[n], :]).then_inc(pT2_ev, 1)
                for f in range(FT):
                    act.wait_ge(up_ps, FT * c + f + 1)
                    nc.scalar.activation(hidden[:, f, :], bank[:, (3, 7)[f % 2], :], ACT.Relu).then_inc(relu2_step, 1)
                    act.wait_ge(relu2_step, FT * c + f + 1)
                    nc.scalar.activation(hidden[:, f, :], hidden[:, f, :], ACT.Square).then_inc(hid_rdy, 1)
                act.wait_ge(ring_used, FT // 2 * (c + 1))
                for a in range(CT):
                    for n in range(2):
                        nc.scalar.activation(junk[:, n * 512:(n + 1) * 512], bank[:, DOWN[n][a], :], ACT.Square,
                                             scale=float(D) ** -0.5, accum_out=ssC[:, n:n + 1]).then_inc(ssC_rdy, 1)
                    act.wait_ge(msC_rdy, 2 * CT * c + a + 1)
                for a in range(CT):
                    i = CT * c + a
                    act.wait_ge(out_step, 2 * i)
                    for n in range(2):
                        act.wait_ge(gate_ps, 2 * i + n + 1)
                        nc.scalar.activation(sig[:, n * 512:(n + 1) * 512], bank[:, (2, 4)[n], :],
                                             ACT.Sigmoid).then_inc(sig_rdy, 1)
                    for n in range(2):
                        act.wait_ge(ge_rdy, 2 * i + n + 1)
                        nc.scalar.activation(junk[:, n * 512:(n + 1) * 512], sig[:, n * 512:(n + 1) * 512], ACT.Square,
                                             scale=float(D) ** -0.5, accum_out=ssC[:, 2 + n:3 + n]).then_inc(ssC_rdy, 1)
                    act.wait_ge(out_step, 2 * i + 2)
                    act.dma_start(out[0, bass.ts(i, P), :], out_t[:]).then_inc(out_st, 16)

            mlp_chunk(0, True)
            with act.Fori(1, NCH) as c:
                mlp_chunk(c, False)

        @block.vector
        def _(dve):
            dve.wait_ge(small_ld, 16 * 5)
            dve.wait_ge(setup_step, 4 + ROT_HALF + G)
            done = [0]

            def link(ins):
                done[0] += 1
                ins.then_inc(rot_setup, 1)
                dve.wait_ge(rot_setup, done[0])

            link(nc.vector.tensor_copy(pos_f[:], pos_i[:]))
            link(nc.vector.tensor_tensor(angle[:], over(pos_f[:], ROT_HALF),
                                         freq[:].unsqueeze(1).to_broadcast([P, T, ROT_HALF]), ALU.mult))
            for n, (quarter, shift) in enumerate(((0.0, 0.0), (0.25, float(np.pi / 2)))):
                link(nc.vector.tensor_scalar(turns[:, n], angle[:], float(1 / (2 * np.pi)), quarter, ALU.mult, ALU.add))
                link(nc.vector.tensor_scalar(turns[:, n], turns[:, n], ROUND, None, ALU.add))
                link(nc.vector.tensor_scalar(turns[:, n], turns[:, n], -ROUND, None, ALU.add))
                rest = angle[:]
                for part in TWO_PI:
                    link(nc.vector.scalar_tensor_tensor(out=trig[:, n], in0=turns[:, n], scalar=float(-part), in1=rest,
                                                        op0=ALU.mult, op1=ALU.add))
                    rest = trig[:, n]
                link(nc.vector.tensor_scalar(turns[:, n], trig[:, n], shift, None, ALU.add))
                link(nc.vector.tensor_scalar(turns[:, n], turns[:, n], PI_SAFE, -PI_SAFE, ALU.min, ALU.max))
            nc.vector.tensor_copy(rot[:, 0, 0:1, 0:1], turns[:, 0, 0:1, 0:1]).then_inc(turns_rdy, 1)

            def norm(i, u):
                dve.wait_ge(ss_rdy, i + 1)
                nc.vector.tensor_scalar(ms[:, u:u + 1], ss[:, u:u + 1], EPS, None, ALU.add).then_inc(ms_rdy, 1)
                dve.wait_ge(rstd_rdy, i + 1)
                nc.vector.tensor_scalar(xn[:], x_in[:, u, :], rstd[:, u:u + 1], None, ALU.mult).then_inc(xn_rdy, 1)

            def evacuate_hnT(i):
                dve.wait_ge(xT_ps, i + 1)
                for n in range(2):
                    nc.vector.tensor_tensor(hnT[:, 4 * n:4 * n + 4, :], split4(bank[:, n, :]),
                                            over(g_pre_col[:, 4 * n:4 * n + 4], P), ALU.mult).then_inc(hnT_rdy, 1)

            def evacuate_k(i):
                dve.wait_ge(k_hi_ev, i + 1)
                cols = bass.ts(i, P)
                nc.vector.tensor_tensor(k_lo[:, :, cols], split4(bank[:, 6, 0:3 * P]), k_hi[:, :, cols].bitcast(F32),
                                        ALU.subtract).then_inc(k_lo_ev, 1)

            def evacuate_y(i):
                dve.wait_ge(y_ps, i + 1)
                dve.wait_ge(pool_st, 16 * i)
                nc.vector.tensor_tensor(y_pool[:], split4(bank[:, 0, :]), over(pool_scale_col[:], P), ALU.mult).then_inc(y_ev, 1)

            def rope(i, u):
                dve.wait_ge(za_ev, i + 1)
                dve.wait_ge(zb_ev, 3 * i + 3)
                dve.wait_ge(zc_ev, 2 * i + 2)
                zb = zs[:, u, :, :]
                x1, x2 = zb[:, :, 0:ROT_HALF], zb[:, :, ROT_HALF:2 * ROT_HALF]
                sin, cos = (trig[:, n, i, :].unsqueeze(1).to_broadcast([P, ZB, ROT_HALF]) for n in range(2))
                for n, (a, b) in enumerate(((x1, cos), (x2, sin), (x2, cos), (x1, sin))):
                    nc.vector.tensor_tensor(rot[:, n], a, b, ALU.mult).then_inc(rot_step, 1)
                dve.wait_ge(rot_step, 6 * i + 4)
                nc.vector.tensor_tensor(x1, rot[:, 0], rot[:, 1], ALU.subtract).then_inc(rot_step, 1)
                nc.vector.tensor_tensor(x2, rot[:, 2], rot[:, 3], ALU.add).then_inc(rot_step, 1)

            def step(i, u, first, last):
                evacuate_hnT(i)
                if not first:
                    evacuate_k(i - 1)
                    evacuate_y(i - 1)
                if not last:
                    norm(i + 1, 1 - u)
                rope(i, u)

            norm(0, 0)
            dve.wait_ge(trig_rdy, 1)
            step(0, 0, True, False)
            step(1, 1, False, False)
            with dve.Fori(0, (T - 4) // 2) as ii:
                step(2 * ii + 2, 0, False, False)
                step(2 * ii + 3, 1, False, False)
            step(T - 2, 0, False, False)
            step(T - 1, 1, False, True)
            evacuate_k(T - 1)
            evacuate_y(T - 1)

            def weigh_scores(g, t, i):
                keys = STEPS[g][3]
                n = 0
                for o, w in blocks_of(keys):
                    for h in range(IDX_HEADS):
                        dve.wait_ge(relu_rdy, idx_n.at(g, t, n + 1))
                        dst, wh = score[:, o:o + w], w_idx[:, i, h:h + 1]
                        if h == 0:
                            nc.vector.tensor_scalar(dst, relu[:, n % 2, 0:w], wh, None, ALU.mult).then_inc(score_step, 1)
                        else:
                            dve.wait_ge(score_step, score_n.at(g, t, n))
                            nc.vector.scalar_tensor_tensor(out=dst, in0=relu[:, n % 2, 0:w], scalar=wh, in1=dst,
                                                           op0=ALU.mult, op1=ALU.add).then_inc(score_step, 1)
                        n += 1
                dve.wait_ge(score_step, score_n.at(g, t, n))
                last = score[:, keys - 2 * P:keys]
                nc.vector.tensor_tensor(last, last, causal[:, bass.ds(P - P * t, 2 * P)], ALU.add).then_inc(score_step, 1)
                dve.wait_ge(score_step, score_n.at(g, t, n + 1))

            def take_top(g, t, rounds):
                keys = STEPS[g][3]
                for r in rounds:
                    src = score if r == 0 else work
                    dve.nop(nofuse=True)
                    nc.vector.max(top8[:], src[:, 0:keys]).then_inc(top_step, 1)
                    dve.wait_ge(top_step, top_n.at(g, t, 2 * r + 1))
                    dve.nop(nofuse=True)
                    nc.vector.match_replace(work[:, 0:keys], top8[:], src[:, 0:keys], TAKEN).then_inc(top_step, 1)
                    dve.wait_ge(top_step, top_n.at(g, t, 2 * r + 2))

            def mask_rest(g, t):
                keys = STEPS[g][3]
                nc.vector.tensor_tensor(work[:, 0:keys], work[:, 0:keys], score[:, 0:keys], ALU.is_equal).then_inc(top_step, 1)
                dve.wait_ge(top_step, top_n.at(g, t, KEEP // 4 + 1))
                nc.vector.tensor_scalar(mask[:, 0:keys], work[:, 0:keys], MASKED, None, ALU.mult).then_inc(mask_rdy, 1)

            def residual(i):
                dve.wait_ge(ssB_rdy, 3 * i + 2)
                nc.vector.tensor_scalar(msB[:, 0:1], ssB[:, 0:1], ssB[:, 1:2], EPS, ALU.add, ALU.add).then_inc(msB_rdy, 1)
                dve.wait_ge(rstdB_rdy, 2 * i + 1)
                dve.wait_ge(h2_st, 16 * i)
                for n in range(2):
                    cols = slice(n * 512, (n + 1) * 512)
                    nc.vector.scalar_tensor_tensor(out=h2_t[:, cols], in0=bank[:, n, :], scalar=rstdB[:, 0:1],
                                                   in1=g_post_row[:, cols], op0=ALU.mult, op1=ALU.mult).then_inc(h2_step, 1)
                dve.wait_ge(h2_step, 3 * i + 2)
                dve.wait_ge(tail_ld, 32 * i + 32)
                nc.vector.tensor_tensor(h2_t[:], h2_t[:], x_t[:], ALU.add).then_inc(h2_step, 1)

            def normalise(i):
                dve.wait_ge(ssB_rdy, 3 * i + 3)
                nc.vector.tensor_scalar(msB[:, 1:2], ssB[:, 2:3], EPS, None, ALU.add).then_inc(msB_rdy, 1)
                dve.wait_ge(rstdB_rdy, 2 * i + 2)
                nc.vector.tensor_scalar(hn2_t[:], h2_t[:], rstdB[:, 1:2], None, ALU.mult).then_inc(hn2_rdy, 1)

            def evacuate_hn2T(i):
                dve.wait_ge(hn2T_ps, i + 1)
                dve.wait_ge(hn2T_st, 16 * i)
                for n in range(2):
                    nc.vector.tensor_tensor(hn2T_t[:, 4 * n:4 * n + 4, :], split4(bank[:, 5 + n, :]),
                                            over(g_mlp_col[:, 4 * n:4 * n + 4], P), ALU.mult).then_inc(hn2T_rdy, 1)

            def mask_head(g, t, i, h):
                blks = blocks_of(STEPS[g][2])
                nb = len(blks)
                dve.wait_ge(pT_ps, head_n.at(g, t, max(h - 1, 0) * nb))
                for b, (o, w) in enumerate(blks):
                    m = h * nb + b
                    dve.wait_ge(s_ps, head_n.at(g, t, m + 1))
                    dve.nop(nofuse=True)
                    nc.vector.tensor_tensor_reduce(out=probs[:, h % 2, o:o + w], in0=bank[:, 2 + m % 3, 0:w],
                                                   in1=mask[:, o:o + w], scale=1.0, scalar=TAKEN, op0=ALU.add,
                                                   op1=ALU.max, accum_out=block_max[:, h % 2, b:b + 1]).then_inc(masked_s, 1)
                dve.wait_ge(masked_s, head_n.at(g, t, (h + 1) * nb))
                nc.vector.tensor_reduce(neg_max[:, h:h + 1], block_max[:, h % 2, 0:nb], AX_X, ALU.max,
                                        negate=True).then_inc(negmax_rdy, 1)

            def outputs(g, t, i):
                dve.wait_ge(pv_ps, head_n.at(g, t, head_n.per[g]))
                nc.vector.reciprocal(inv_denom[:], denom[:]).then_inc(invden_rdy, 1)
                dve.wait_ge(invden_rdy, i + 1)
                nc.vector.tensor_tensor(o_sb[:], bank[:, 7, :].rearrange("p (h d) -> p h d", d=HEAD),
                                        over(inv_denom[:], HEAD), ALU.mult).then_inc(o_rdy, 1)

            def split_queries(i, indexer):
                low = slice(P // 2, P)
                if indexer:
                    dve.wait_ge(qi_hi, i)
                    part = q_parts[low, Q_HEADS:, :]
                    nc.vector.tensor_tensor(part, split4(bank[low, 2, :]), part.bitcast(F32), ALU.subtract).then_inc(qi_lo, 1)
                dve.wait_ge(q_hi, 2 * i + 2)
                for n in range(2):
                    part = q_parts[low, 4 * n:4 * n + 4, :]
                    nc.vector.tensor_tensor(part, split4(bank[low, 5 + n, :]), part.bitcast(F32), ALU.subtract).then_inc(q_lo, 1)

            def attn_step(g, t, i):
                picking = top_blocks[g] > 0
                rounds = range(KEEP // 8 if picking else 0)
                split_queries(i, picking)
                if picking:
                    weigh_scores(g, t, i + 1)
                if g > 0:
                    residual(i - 1)
                take_top(g, t, rounds[:2])
                if g > 0:
                    normalise(i - 1)
                take_top(g, t, rounds[2:5])
                if g > 0:
                    evacuate_hn2T(i - 1)
                take_top(g, t, rounds[5:8])
                for h in range(Q_HEADS):
                    mask_head(g, t, i, h)
                    take_top(g, t, rounds[8 + 3 * h:11 + 3 * h])
                if picking:
                    mask_rest(g, t)
                elif STEPS[g][3]:
                    nc.vector.tensor_copy(mask[:, 0:2 * P], causal[:, 0:2 * P]).then_inc(mask_rdy, 1)
                outputs(g, t, i)

            dve.wait_ge(mixer_step, 10 * T)
            dve.wait_ge(const_rdy, sum(WINDOWS) - G + 2)
            dve.wait_ge(q_st[0], 8 * T)
            dve.wait_ge(q_st[1], 8 * T)
            dve.wait_ge(pool_st, 16 * T)
            dve.wait_ge(wo_ld, 16 * (K + 1))
            nc.vector.memset(mask[:], MASKED).then_inc(mask_rdy, 1)
            dve.wait_ge(mask_rdy, 1)
            nc.vector.tensor_copy(mask[:, 0:P], causal[:, P:2 * P]).then_inc(mask_rdy, 1)
            dve.wait_ge(mask_rdy, 2)
            for g, (i0, n, _, _) in enumerate(STEPS):
                if g < 2 or n == 1:
                    for t in range(n):
                        attn_step(g, t, i0 + t)
                        dve.wait_ge(mask_rdy, min(i0 + t + 3, T + 1))
                else:
                    with dve.Fori(0, n) as t:
                        attn_step(g, t, i0 + t)
                        dve.wait_ge(mask_rdy, i0 + t + 3)
                        dve.nop(nofuse=True)
            residual(T - 1)
            normalise(T - 1)
            evacuate_hn2T(T - 1)

            dve.wait_ge(wc_ld, 16 * (K + KP + 2))

            def mlp_chunk(c, first):
                dve.wait_ge(h2_ld, 16 * c + 16)
                for a in range(CT):
                    i = CT * c + a
                    dve.wait_ge(ssC_rdy, 4 * CT * c + 2 * a + 2)
                    nc.vector.tensor_scalar(msC[:, 0:1], ssC[:, 0:1], ssC[:, 1:2], EPS, ALU.add, ALU.add).then_inc(msC_rdy, 1)
                    dve.wait_ge(rstdC_rdy, 2 * CT * c + a + 1)
                    for n in range(2):
                        cols = slice(n * 512, (n + 1) * 512)
                        nc.vector.scalar_tensor_tensor(out=m_t[:, cols], in0=bank[:, DOWN[n][a], :], scalar=rstdC[:, 0:1],
                                                       in1=g_mlp_row[:, cols], op0=ALU.mult, op1=ALU.mult).then_inc(m_step, 1)
                    dve.wait_ge(m_step, 3 * i + 2)
                    nc.vector.tensor_tensor(h2[:, a, :], h2[:, a, :], m_t[:], ALU.add).then_inc(m_step, 1)
                for a in range(CT):
                    i = CT * c + a
                    dve.wait_ge(h3T_ps, i + 1)
                    for n in range(2):
                        nc.vector.tensor_copy(h3T[:, 4 * n:4 * n + 4, :], split4(bank[:, (0, 5)[n], :])).then_inc(h3T_rdy, 1)
                    dve.wait_ge(e_ps, i + 1)
                    for n in range(2):
                        cols = slice(n * 512, (n + 1) * 512)
                        dve.wait_ge(sig_rdy, 2 * i + n + 1)
                        nc.vector.tensor_tensor(sig[:, cols], bank[:, (1, 6)[n], :], sig[:, cols], ALU.mult).then_inc(ge_rdy, 1)
                    dve.wait_ge(ssC_rdy, 4 * CT * c + 2 * CT + 2 * a + 2)
                    nc.vector.tensor_scalar(msC[:, 1:2], ssC[:, 2:3], ssC[:, 3:4], EPS, ALU.add, ALU.add).then_inc(msC_rdy, 1)
                    dve.wait_ge(rstdC_rdy, 2 * CT * c + CT + a + 1)
                    dve.wait_ge(out_st, 16 * i)
                    nc.vector.scalar_tensor_tensor(out=out_t[:], in0=sig[:], scalar=rstdC[:, 1:2], in1=g_ple_row[:],
                                                   op0=ALU.mult, op1=ALU.mult).then_inc(out_step, 1)
                    dve.wait_ge(out_step, 2 * i + 1)
                    nc.vector.tensor_tensor(out_t[:], out_t[:], h2[:, a, :], ALU.add).then_inc(out_step, 1)

            mlp_chunk(0, True)
            with dve.Fori(1, NCH) as c:
                mlp_chunk(c, False)

        @block.tensor
        def _(pe):
            pe.wait_ge(const_rdy, sum(WINDOWS) - G + 2)
            pe.wait_ge(small_ld, 16 * 5)

            def transposes(banks, src, done_sem):
                for n, b in enumerate(banks):
                    for a in range(4):
                        k = 4 * n + a
                        last = nc.tensor.transpose(bank[:, b, a * P:(a + 1) * P], src[:, k * P:(k + 1) * P], ident[:])
                last.then_inc(done_sem, 1)

            def transpose_x(i, first):
                pe.wait_ge(xn_rdy, i + 1)
                if not first:
                    pe.wait_ge(y_ev, i - 1)
                transposes((0, 1), xn, xT_ps)

            def transpose_k(i, u):
                pe.wait_ge(rot_step, 6 * i + 6)
                pe.wait_ge(k_lo_ev, i)
                for n in range(3):
                    last = nc.tensor.transpose(bank[:, 6, n * P:(n + 1) * P],
                                               zs[:, u, 12 + 2 * n:14 + 2 * n, :].rearrange("p a d -> p (a d)"), ident[:])
                last.then_inc(kT_ps, 1)

            def pool_product(i):
                pe.wait_ge(mixer_step, 10 * i + 9)
                for g in range(G):
                    last = nc.tensor.matmul(bank[:, 0, g * P:(g + 1) * P], w_pool_sb[:, g, :], r_pool[:, g, :],
                                            start=True, stop=True)
                last.then_inc(y_ps, 1)

            def project(i):
                for b, (lo, hi), ev, per, ps in ((2, (0, Z_A), za_ev, 1, za_ps), (3, (Z_A, Z_B), zb_ev, 3, zb_ps),
                                                 (4, (Z_B, Z_POOL), zc_ev, 2, zc_ps)):
                    pe.wait_ge(ev, per * i)
                    for k in range(K):
                        last = nc.tensor.matmul(bank[:, b, 0:hi - lo], hnT[:, k, :], w_in_sb[:, k, lo:hi],
                                                start=(k == 0), stop=(k == K - 1))
                    last.then_inc(ps, 1)
                pe.wait_ge(zp_ev, i)
                for g in range(G):
                    for k in range(K):
                        last = nc.tensor.matmul(bank[:, 5, g * P:(g + 1) * P],
                                                w_in_sb[:, k, Z_POOL + g * P:Z_POOL + (g + 1) * P], hnT[:, k, :],
                                                start=(k == 0), stop=(k == K - 1))
                last.then_inc(zp_ps, 1)

            def step(i, u, first):
                transpose_x(i, first)
                if not first:
                    transpose_k(i - 1, 1 - u)
                pe.wait_ge(hnT_rdy, 2 * i + 2)
                if not first:
                    pool_product(i - 1)
                project(i)

            pe.wait_ge(w_in_ld, 16 * K)
            step(0, 0, True)
            step(1, 1, False)
            with pe.Fori(0, (T - 2) // 2) as ii:
                step(2 * ii + 2, 0, False)
                step(2 * ii + 3, 1, False)
            transpose_k(T - 1, 1)
            pool_product(T - 1)

            for s, n in ((za_ev, 1), (zb_ev, 3), (zc_ev, 2), (zp_ev, 1), (k_hi_ev, 1), (k_lo_ev, 1), (y_ev, 1), (mixer_step, 10)):
                pe.wait_ge(s, n * T)
            pe.wait_ge(wo_ld, 16 * (K + 1))

            def turn_queries(i, indexer):
                if indexer:
                    pe.wait_ge(qi_ld, 32 * i)
                    for h in range(IDX_HEADS):
                        last = nc.tensor.transpose(bank[:, 2, h * P:(h + 1) * P],
                                                   q_t[:, Q_HEADS + h].rearrange("p e d -> p (e d)"), ident[:])
                    last.then_inc(qiT_ps, 1)
                pe.wait_ge(q_ld, 32 * i + 32)
                for h in range(Q_HEADS):
                    last = nc.tensor.transpose(bank[:, 5 + h // 4, (h % 4) * P:(h % 4 + 1) * P],
                                               q_t[:, h].rearrange("p e d -> p (e d)"), ident[:])
                last.then_inc(qT_ps, 1)

            def exact_product(dst, q, key, o, w):
                nc.tensor.matmul(dst, q_parts[:, q, :], k_hi[:, key, o:o + w], start=True, stop=False)
                return nc.tensor.matmul(dst, q_parts[:, q, :], k_lo[:, key, o:o + w], start=False, stop=True)

            def index(g, t, i):
                pe.wait_ge(qi_lo, i)
                n = 0
                for o, w in blocks_of(STEPS[g][3]):
                    for h in range(IDX_HEADS):
                        if n >= 2:
                            pe.wait_ge(relu_rdy, idx_n.at(g, t, n - 1))
                        exact_product(bank[:, n % 2, 0:w], Q_HEADS + h, 2, o, w).then_inc(idx_ps, 1)
                        n += 1
                pe.wait_ge(relu_rdy, idx_n.at(g, t, n))

            def output_projection(i):
                pe.wait_ge(o_rdy, i + 1)
                transposes((5,), o_sb[:].rearrange("p h d -> p (h d)"), oT_ps)
                pe.wait_ge(mixT_rdy, i + 1)
                pe.wait_ge(tail_ld, 32 * i + 32)
                for n in range(2):
                    for k in range(K):
                        last = nc.tensor.matmul(bank[:, n, :], mixT_t[:, k, :], wo_sb[:, k, n * 512:(n + 1) * 512],
                                                start=(k == 0), stop=(k == K - 1))
                last.then_inc(wo_ps, 1)

            def transpose_hn2(i):
                pe.wait_ge(hn2_rdy, i + 1)
                transposes((5, 6), hn2_t, hn2T_ps)
                pe.wait_ge(hn2T_rdy, 2 * i + 2)

            def attend(g, t, i):
                keys = STEPS[g][2]
                blks = blocks_of(keys)
                nb = len(blks)

                def scores(h):
                    for b, (o, w) in enumerate(blks):
                        m = h * nb + b
                        if m >= 3:
                            pe.wait_ge(masked_s, head_n.at(g, t, m - 2))
                        exact_product(bank[:, 2 + m % 3, 0:w], h, h // (Q_HEADS // KV_HEADS), o, w).then_inc(s_ps, 1)

                def weigh(h, b):
                    o, w = blks[b]
                    m = h * nb + b
                    kv = h // (Q_HEADS // KV_HEADS)
                    pe.wait_ge(pT_ev, head_n.at(g, t, m + 1))
                    for a in range(w // P):
                        kt = o // P + a
                        last = nc.tensor.matmul(bank[:, 7, h * HEAD:(h + 1) * HEAD], probsT[:, m % 2, a * P:(a + 1) * P],
                                                values[:, kt, HEAD * kv:HEAD * (kv + 1)],
                                                start=(kt == 0), stop=(kt == keys // P - 1))
                    last.then_inc(pv_ps, 1)

                scores(0)
                for h in range(Q_HEADS):
                    if h + 1 < Q_HEADS:
                        scores(h + 1)
                    pe.wait_ge(exp_rdy, Q_HEADS * i + h + 1)
                    for b, (o, w) in enumerate(blks):
                        m = h * nb + b
                        if m >= 2:
                            pe.wait_ge(pT_ev, head_n.at(g, t, m - 1))
                        for a in range(w // P):
                            last = nc.tensor.transpose(bank[:, 5 + m % 2, a * P:(a + 1) * P],
                                                       probs[:, h % 2, o + a * P:o + (a + 1) * P], ident[:])
                        last.then_inc(pT_ps, 1)
                        if b > 0:
                            weigh(h, b - 1)
                    weigh(h, nb - 1)

            def attn_step(g, t, i):
                turn_queries(i, top_blocks[g] > 0)
                if top_blocks[g]:
                    index(g, t, i)
                pe.wait_ge(q_lo, 2 * i + 2)
                if g > 0:
                    output_projection(i - 1)
                    transpose_hn2(i - 1)
                attend(g, t, i)

            for g, (i0, n, _, _) in enumerate(STEPS):
                if g < 2 or n == 1:
                    for t in range(n):
                        attn_step(g, t, i0 + t)
                else:
                    with pe.Fori(0, n) as t:
                        attn_step(g, t, i0 + t)
            output_projection(T - 1)
            transpose_hn2(T - 1)

            pe.wait_ge(wc_ld, 16 * (K + KP + 2))

            def mlp_chunk(c, first):
                pe.wait_ge(m_step, 3 * CT * c)
                pe.wait_ge(p_ld, 16 * c + 16)
                for k in range(KP):
                    for a in range(CT):
                        last = nc.tensor.transpose(bank[:, (3, 7)[k], a * P:(a + 1) * P], p_in[:, a, k * P:(k + 1) * P], ident[:])
                    last.then_inc(pT2_ps, 1)

                def weights(s):
                    pe.wait_ge(ring_ld[s % 4], 16 * (8 * c + s // 4 + 1))
                    return ring[:, s % 4, :]

                pe.wait_ge(hn2T_ld, 16 * c + 16)
                for f in range(FT):
                    if f % 2 == 0:
                        slot = weights(f // 2).rearrange("p (k f) -> p k f", f=256)
                    if f < 2:
                        pe.wait_ge(pT2_ev, 2 * c + f + 1)
                    else:
                        pe.wait_ge(relu2_step, FT * c + f - 1)
                    for k in range(K):
                        last = nc.tensor.matmul(bank[:, (3, 7)[f % 2], :], slot[:, k, (f % 2) * P:(f % 2 + 1) * P],
                                                hn2T[:, k, :], start=(k == 0), stop=(k == K - 1))
                    last.then_inc(up_ps, 1)

                pe.wait_ge(hid_rdy, FT * (c + 1))
                pe.wait_ge(h3T_rdy, 2 * CT * c)
                pe.wait_ge(ge_rdy, 2 * CT * c)
                pe.wait_ge(sig_rdy, 2 * CT * c)
                for half in range(2):
                    for q in range(8):
                        slot = weights(16 + 8 * half + q).rearrange("p (a d) -> p a d", d=512)
                        for r in range(4):
                            f = 4 * q + r
                            for a in range(CT):
                                last = nc.tensor.matmul(bank[:, DOWN[half][a], :], hidden[:, f, a * P:(a + 1) * P],
                                                        slot[:, r, :], start=(f == 0), stop=(f == FT - 1))
                        last.then_inc(ring_used, 1)

                for a in range(CT):
                    i = CT * c + a
                    pe.wait_ge(m_step, 3 * i + 3)
                    pe.wait_ge(h3T_rdy, 2 * i)
                    transposes((0, 5), h2[:, a, :], h3T_ps)
                    if a == 0:
                        pe.wait_ge(m_step, 3 * i + 6)
                    pe.wait_ge(ge_rdy, 2 * i)
                    for n in range(2):
                        for k in range(KP):
                            last = nc.tensor.matmul(bank[:, (1, 6)[n], :], pT[:, k, a * P:(a + 1) * P],
                                                    w_ple_sb[:, k, n * 512:(n + 1) * 512], start=(k == 0), stop=(k == KP - 1))
                    last.then_inc(e_ps, 1)
                    if a == 0:
                        pe.wait_ge(m_step, 3 * i + 12)
                    pe.wait_ge(h3T_rdy, 2 * i + 2)
                    pe.wait_ge(sig_rdy, 2 * i)
                    for n in range(2):
                        for k in range(K):
                            last = nc.tensor.matmul(bank[:, (2, 4)[n], :], h3T[:, k, :],
                                                    w_gate_sb[:, k, n * 512:(n + 1) * 512], start=(k == 0), stop=(k == K - 1))
                        last.then_inc(gate_ps, 1)

            mlp_chunk(0, True)
            with pe.Fori(1, NCH) as c:
                mlp_chunk(c, False)


_INS = ["x", "p", "positions", "g_mix_pre", "w_in", "w_pool", "pool_scale", "w_o", "g_mix_post",
        "g_mlp_pre", "w_up", "w_down", "g_mlp_post", "w_ple_gate", "w_ple_proj", "g_ple_post"]


def kernel(**inputs):
    import concourse.bacc as bacc
    from concourse.bass_utils import run_bass_kernel_spmd

    nc = bacc.Bacc("TRN2", target_bir_lowering=False, num_devices=1)
    arrays, args = {}, []
    for name in _INS:
        a = np.ascontiguousarray(inputs[name])
        arrays[f"in_{name}"] = a
        args.append(nc.dram_tensor(f"in_{name}", a.shape, mybir.dt.from_np(a.dtype), kind="ExternalInput").ap())
    shape = arrays["in_x"].shape
    args.append(nc.dram_tensor("out_h", shape, F32, kind="ExternalOutput").ap())
    hybrid_block(nc, *args)
    r = run_bass_kernel_spmd(nc, [arrays], core_ids=[0])
    return r.results[0]["out_h"]
```
